# Optimizing a Trainium2 kernel written in Bass

```python
import math
import jax, jax.numpy as jnp
from jax import lax
import numpy as np

D_MODEL = 1024
BATCH = 1
SEQ = 256
DEPTH = 2

CHUNK = 64
PLE_DIM = 256
D_FF = 2816
EPS = 1e-6
N_NORMS = 8

SSM_HEADS = 16
SSM_HEAD_DIM = 64
SSM_D_INNER = SSM_HEADS * SSM_HEAD_DIM
SSM_GROUPS = 2
SSM_STATE = 128
CONV_WIDTH = 4
CONV_DIM = SSM_D_INNER + 2 * SSM_GROUPS * SSM_STATE

ATTN_HEADS = 16
ATTN_KV_HEADS = 4
ATTN_HEAD_DIM = 64
ATTN_D = ATTN_HEADS * ATTN_HEAD_DIM
KV_D = ATTN_KV_HEADS * ATTN_HEAD_DIM
WINDOW = 128
WINDOW_CHUNKS = WINDOW // CHUNK
N_BUCKETS = 32
MAX_DISTANCE = 128

D_MIX = SSM_D_INNER + ATTN_D
IN_SPLITS = (SSM_D_INNER, CONV_DIM, SSM_HEADS, ATTN_D, KV_D, KV_D)
D_IN_PROJ = sum(IN_SPLITS)

kernel_name = "hymba_ssd_swa_sink_macaron_stream"

def _rmsnorm(t, w):
    tf = t.astype(jnp.float32)
    tf = tf * lax.rsqrt(jnp.mean(tf * tf, axis=-1, keepdims=True) + EPS)
    return (tf * w.astype(jnp.float32)).astype(t.dtype)

def _swiglu(u, w13, w2):
    a, g = jnp.split(u @ w13, 2, axis=-1)
    return (jax.nn.silu(a) * g) @ w2

def _t5_buckets():
    qi = np.arange(CHUNK)[:, None]
    kj = np.arange(WINDOW_CHUNKS * CHUNK)[None, :]
    rel = kj - (WINDOW_CHUNKS - 1) * CHUNK - qi
    nb = N_BUCKETS // 2
    ret = (rel > 0).astype(np.int32) * nb
    n = np.abs(rel)
    max_exact = nb // 2
    large = max_exact + (np.log(np.maximum(n, 1) / max_exact)
                         / np.log(MAX_DISTANCE / max_exact) * (nb - max_exact)).astype(np.int32)
    large = np.minimum(large, nb - 1)
    return (ret + np.where(n < max_exact, n, large)).astype(np.int32)

def _causal_dwconv(t, w, b):
    s = t.shape[1]
    tp = jnp.pad(t, ((0, 0), (CONV_WIDTH - 1, 0), (0, 0)))
    return sum(tp[:, k:k + s] * w[k] for k in range(CONV_WIDTH)) + b

def _ssd(xh, dt, a, bm, cm):
    b, s = xh.shape[:2]
    nc = s // CHUNK
    e = SSM_HEADS // SSM_GROUPS
    f32 = jnp.float32
    X = (xh.astype(f32) * dt[..., None]).reshape(b, nc, CHUNK, SSM_GROUPS, e, SSM_HEAD_DIM)
    Adt = (dt * a).reshape(b, nc, CHUNK, SSM_GROUPS, e)
    Bc = bm.astype(f32).reshape(b, nc, CHUNK, SSM_GROUPS, SSM_STATE)
    Cc = cm.astype(f32).reshape(b, nc, CHUNK, SSM_GROUPS, SSM_STATE)
    cs = jnp.cumsum(Adt, axis=2)
    seg = cs[:, :, :, None] - cs[:, :, None, :]
    causal = jnp.tril(jnp.ones((CHUNK, CHUNK), dtype=bool))[None, None, :, :, None, None]
    L = jnp.exp(jnp.where(causal, seg, -jnp.inf))
    CB = jnp.einsum('bclgn,bcsgn->bclsg', Cc, Bc)
    y_diag = jnp.einsum('bclsge,bcsgep->bclgep', CB[..., None] * L, X)
    Xd = X * jnp.exp(cs[:, :, -1:] - cs)[..., None]
    states = jnp.einsum('bclgn,bclgep->bcgepn', Bc, Xd)
    chunk_decay = jnp.exp(cs[:, :, -1])

    def step(h, inp):
        st, dec = inp
        return h * dec[..., None, None] + st, h

    h0 = jnp.zeros((b, SSM_GROUPS, e, SSM_HEAD_DIM, SSM_STATE), f32)
    _, h_in = lax.scan(step, h0, (jnp.swapaxes(states, 0, 1), jnp.swapaxes(chunk_decay, 0, 1)))
    h_in = jnp.swapaxes(h_in, 0, 1)
    y_off = jnp.einsum('bclgn,bcgepn->bclgep', Cc, h_in) * jnp.exp(cs)[..., None]
    return (y_diag + y_off).reshape(b, s, SSM_HEADS, SSM_HEAD_DIM)

def _swa_sink_attention(q, k, v, rel_bias, sinks):
    b, s = q.shape[:2]
    nc = s // CHUNK
    g = ATTN_HEADS // ATTN_KV_HEADS
    wc = WINDOW_CHUNKS * CHUNK
    qc = q.reshape(b, nc, CHUNK, ATTN_KV_HEADS, g, ATTN_HEAD_DIM)

    def window(t):
        tc = t.reshape(b, nc, CHUNK, ATTN_KV_HEADS, ATTN_HEAD_DIM)
        tp = jnp.pad(tc, ((0, 0), (WINDOW_CHUNKS - 1, 0), (0, 0), (0, 0), (0, 0)))
        return jnp.concatenate([tp[:, j:j + nc] for j in range(WINDOW_CHUNKS)], axis=2)

    kw, vw = window(k), window(v)
    scale = 1.0 / math.sqrt(ATTN_HEAD_DIM)
    logits = jnp.einsum('bcqkgd,bcjkd->bckgqj', qc, kw).astype(jnp.float32) * scale
    logits = logits + rel_bias.astype(jnp.float32)[None, None]
    key_chunk = (jnp.arange(nc)[:, None] - (WINDOW_CHUNKS - 1)
                 + (jnp.arange(wc) // CHUNK)[None, :])
    valid = (key_chunk >= 0)[None, :, None, None, None, :]
    logits = jnp.where(valid, logits, -jnp.inf)
    sink = jnp.broadcast_to(
        sinks.astype(jnp.float32).reshape(ATTN_KV_HEADS, g)[None, None, :, :, None, None],
        logits.shape[:-1] + (1,))
    probs = jax.nn.softmax(jnp.concatenate([logits, sink], axis=-1), axis=-1)[..., :-1]
    out = jnp.einsum('bckgqj,bcjkd->bcqkgd', probs.astype(vw.dtype), vw)
    return out.reshape(b, s, ATTN_D)

def _token_mixer(u, w_in, conv_w, conv_b, dt_bias, a_log, d_skip, ssm_norm_w,
                 sinks, rel_bias, w_out):
    b, s = u.shape[:2]
    z, xbc, dt_raw, q, k, v = jnp.split(u @ w_in, np.cumsum(IN_SPLITS)[:-1].tolist(), axis=-1)
    xbc = jax.nn.silu(_causal_dwconv(xbc, conv_w, conv_b))
    xs, bm, cm = jnp.split(xbc, [SSM_D_INNER, SSM_D_INNER + SSM_GROUPS * SSM_STATE], axis=-1)
    xh = xs.reshape(b, s, SSM_HEADS, SSM_HEAD_DIM)
    dt = jax.nn.softplus(dt_raw.astype(jnp.float32) + dt_bias.astype(jnp.float32))
    a = -jnp.exp(a_log.astype(jnp.float32))
    y = _ssd(xh, dt, a,
             bm.reshape(b, s, SSM_GROUPS, SSM_STATE), cm.reshape(b, s, SSM_GROUPS, SSM_STATE))
    y = (y + d_skip.astype(jnp.float32)[:, None] * xh.astype(jnp.float32)).astype(u.dtype)
    y_ssd = _rmsnorm(y.reshape(b, s, SSM_D_INNER) * jax.nn.silu(z), ssm_norm_w)
    y_att = _swa_sink_attention(q, k, v, rel_bias, sinks)
    return jnp.concatenate([y_ssd, y_att], axis=-1) @ w_out

def setup_inputs(seed: int = 0) -> dict:
    key = jax.random.key(seed)
    ks = jax.random.split(key, 20)
    f32 = jnp.float32
    nrm = lambda k, shape, fan: jax.random.normal(k, shape, f32) * fan ** -0.5
    dt0 = jnp.exp(jax.random.uniform(ks[8], (DEPTH, SSM_HEADS), f32,
                                     math.log(1e-3), math.log(1e-1)))
    return {
        "x": jax.random.normal(ks[0], (BATCH, SEQ, D_MODEL), f32),
        "p": jax.random.normal(ks[1], (DEPTH, BATCH, SEQ, PLE_DIM), f32),
        "norm_w": 1.0 + 0.05 * jax.random.normal(ks[2], (DEPTH, N_NORMS, D_MODEL), f32),
        "ffn1_w13": nrm(ks[3], (DEPTH, D_MODEL, 2 * D_FF), D_MODEL),
        "ffn1_w2": nrm(ks[4], (DEPTH, D_FF, D_MODEL), D_FF),
        "ffn2_w13": nrm(ks[5], (DEPTH, D_MODEL, 2 * D_FF), D_MODEL),
        "ffn2_w2": nrm(ks[6], (DEPTH, D_FF, D_MODEL), D_FF),
        "w_in": nrm(ks[7], (DEPTH, D_MODEL, D_IN_PROJ), D_MODEL),
        "conv_w": nrm(ks[9], (DEPTH, CONV_WIDTH, CONV_DIM), CONV_WIDTH),
        "conv_b": 0.02 * jax.random.normal(ks[10], (DEPTH, CONV_DIM), f32),
        "dt_bias": dt0 + jnp.log(-jnp.expm1(-dt0)),
        "a_log": jnp.log(jax.random.uniform(ks[11], (DEPTH, SSM_HEADS), f32, 1.0, 16.0)),
        "d_skip": 1.0 + 0.1 * jax.random.normal(ks[12], (DEPTH, SSM_HEADS), f32),
        "ssm_norm_w": 1.0 + 0.05 * jax.random.normal(ks[13], (DEPTH, SSM_D_INNER), f32),
        "attn_sinks": 0.5 * jax.random.normal(ks[14], (DEPTH, ATTN_HEADS), f32),
        "rel_bias_table": 0.5 * jax.random.normal(ks[15], (N_BUCKETS, ATTN_HEADS), f32),
        "w_out": nrm(ks[16], (DEPTH, D_MIX, D_MODEL), D_MIX),
        "ple_w_gate": nrm(ks[17], (DEPTH, D_MODEL, D_MODEL), D_MODEL),
        "ple_w_proj": nrm(ks[18], (DEPTH, PLE_DIM, D_MODEL), PLE_DIM),
    }

def reference(x, p, norm_w, ffn1_w13, ffn1_w2, ffn2_w13, ffn2_w2, w_in, conv_w, conv_b,
              dt_bias, a_log, d_skip, ssm_norm_w, attn_sinks, rel_bias_table, w_out,
              ple_w_gate, ple_w_proj):
    g = ATTN_HEADS // ATTN_KV_HEADS
    rel_bias = jnp.transpose(rel_bias_table[_t5_buckets()], (2, 0, 1)).reshape(
        ATTN_KV_HEADS, g, CHUNK, WINDOW_CHUNKS * CHUNK)
    for i in range(DEPTH):
        nw = norm_w[i]
        x = x + 0.5 * _rmsnorm(_swiglu(_rmsnorm(x, nw[0]), ffn1_w13[i], ffn1_w2[i]), nw[1])
        mix = _token_mixer(_rmsnorm(x, nw[2]), w_in[i], conv_w[i], conv_b[i], dt_bias[i],
                           a_log[i], d_skip[i], ssm_norm_w[i], attn_sinks[i], rel_bias, w_out[i])
        x = x + _rmsnorm(mix, nw[3])
        x = x + 0.5 * _rmsnorm(_swiglu(_rmsnorm(x, nw[4]), ffn2_w13[i], ffn2_w2[i]), nw[5])
        gate = jax.nn.sigmoid(_rmsnorm(x, nw[6]) @ ple_w_gate[i])
        x = x + _rmsnorm(gate * (p[i] @ ple_w_proj[i]), nw[7])
    return x


_drawn_inputs = setup_inputs


def setup_inputs(seed=0):
    import zlib

    import numpy as np

    out = dict(_drawn_inputs(seed))
    spreads = {}
    factors = {'attn_sinks': 8.0}
    for name, (base, spread) in spreads.items():
        noise = np.random.default_rng([zlib.crc32(name.encode()), seed]).standard_normal(out[name].shape)
        drawn = base * np.exp(spread * noise) if base else spread * noise
        out[name] = __import__('jax').numpy.asarray(drawn.astype(out[name].dtype))
    for name, factor in factors.items():
        out[name] = (out[name] * factor).astype(out[name].dtype)
    return out
```

```python
import math
from contextlib import ExitStack

import numpy as np
import concourse.bass as bass
from concourse import mybir

F32 = mybir.dt.float32
F32R = mybir.dt.float32r
ALU = mybir.AluOpType
ACT = mybir.ActivationFunctionType
AX = mybir.AxisListType.X

P = 128
D = 1024
SEQ = 256
DEPTH = 2
TT = SEQ // P
KT = D // P
D_FF = 2816
HT = D_FF // P
FW = 256
GROUPS = D_FF // FW
PLE = 256
EPS = 1e-6
NORMS = 8
CHUNK = 64
HEADS = 16
HD = 64
STATE = 128
CONVW = 4
CT = 12
KV = 4
BUCKETS = 32
WIN = 128
SCALE = 1.0 / math.sqrt(HD)
MASKED = -1.0e30

CW = 2048
RING = 4
C_FFN1 = 0
C_DOWN1 = C_FFN1 + 2 * GROUPS
C_Q = C_DOWN1 + HT // 2
C_KV = C_Q + 4
C_XBC = C_KV + 2
C_DT = C_XBC + 6
C_Z = C_DT + 1
C_OUT_ATT = C_Z + 4
C_OUT_SSD = C_OUT_ATT + 4
C_FFN2 = C_OUT_SSD + 4
C_DOWN2 = C_FFN2 + 2 * GROUPS
C_PLE = C_DOWN2 + HT // 2
C_GATE = C_PLE + 1
CHUNKS = C_GATE + 4
AHEAD = 3
assert CHUNKS % RING == 0
LOADS = CHUNKS // RING

K_ID, K_TRI, K_BLK, K_HALF, K_ONEHOT = 0, P, 2 * P, 3 * P, 3 * P + 2
K_ALL = K_ONEHOT + 191

A_CW, A_CB, A_DTB, A_ALOG, A_DSKIP, A_SINK = 0, 48, 60, 76, 92, 108
A_ALL = 124

N_T0 = 2 * (GROUPS + 1) + 2 + 1 + 1 + 1
N_NORM = 18
N_UT = 10
N_X = 2 * 4
N_WIN = 9
N_H = 2 * 2 * GROUPS
N_HT = 2 * GROUPS
N_ITEM = TT * KV

T0_FFN = (0, GROUPS + 4)
T0_DOWN = (GROUPS, 2 * GROUPS + 4)
T0_Z = GROUPS + 1
T0_OUT = GROUPS + 3
T0_PLE = 2 * GROUPS + 5
T0_GATE = 2 * GROUPS + 6
assert T0_GATE + 1 == N_T0

ROW_SSM = NORMS
ROW_SLOT = {0: 0, 1: 1, 2: 0, ROW_SSM: 1, 3: 0, 4: 1, 5: 0, 6: 1, 7: 0}
ROW_LOADS = {0: 5, 1: 4}
ROW_NTH = {0: 1, 2: 2, 3: 3, 5: 4, 7: 5, 1: 1, ROW_SSM: 2, 4: 3, 6: 4}


def trunk(nc, x_in, chunks_in, ple_in, rows_in, params_in, table_in, consts_in, out):
    ctx = ExitStack()
    with ctx:
        at = {"o": -(-nc.sbuf_base // 64) * 64}

        def place(name, cols, dt=F32, offset=None):
            o = at["o"] if offset is None else offset
            t = nc.alloc_sbuf_tensor_at(name, [P, cols], dt, offset=o)
            if offset is None:
                at["o"] = o + -(-cols * 4 // 32) * 32
            return t

        def sem(name):
            return ctx.enter_context(nc.semaphore(name))

        stage = [place(f"stage{s}", CW) for s in range(RING)]
        w_hi = [place(f"w_hi{s}", CW, F32R) for s in range(RING)]
        w_lo = [place(f"w_lo{s}", CW, F32R) for s in range(RING)]
        x_sb = place("x_sb", TT * D)[:].rearrange("p (t n) -> p t n", t=TT)
        tm = place("tm", TT * D)[:].rearrange("p (t n) -> p t n", t=TT)
        uT_hi_t = place("uT_hi", KT * SEQ, F32R)
        uT_lo_t = place("uT_lo", KT * SEQ, F32R)
        rows = [place(f"row{s}", D) for s in range(2)]
        bias = place("bias", HEADS * WIN)[:].rearrange("p (h j) -> p h j", h=HEADS)
        consts = place("consts", K_ALL)
        params = place("params", A_ALL)
        table = place("table", HEADS)
        ss = place("ss", 2 * TT)
        var = place("var", 2 * TT)
        rstd = place("rstd", 2 * TT)
        half_neg = place("half_neg", 1)
        soft = place("soft", 16)
        dts = place("dts", 10 * 32)
        att_s = place("att_s", 2 * 5 * KV)
        region = at["o"]
        hT_hi_t = place("hT_hi", HT * SEQ, F32R, region)
        hT_lo_t = place("hT_lo", HT * SEQ, F32R, region + HT * SEQ * 4)
        sg_t = place("sg", 2 * TT * FW, F32, region + 2 * HT * SEQ * 4)
        hs_t = place("hs", 2 * TT * FW, F32, region + 2 * HT * SEQ * 4 + 2 * TT * FW * 4)
        pw_t = place("pw", TT * D, F32, region)
        ple_raw_t = place("ple_raw", 2 * SEQ, F32, region + 2 * HT * SEQ * 4 + 4 * TT * FW * 4)
        ple_hi_t = place("ple_hi", 2 * SEQ, F32R, region + 2 * HT * SEQ * 4 + 4 * TT * FW * 4 + 2 * SEQ * 4)
        ple_lo_t = place("ple_lo", 2 * SEQ, F32R, region + 2 * HT * SEQ * 4 + 4 * TT * FW * 4 + 4 * SEQ * 4)
        mix_cols = CT * SEQ + 2048 + 1024 + 2048 + 2048 + 1024 + 2048
        mix = place("mix", mix_cols, F32, region)
        attT_hi_t = place("attT_hi", KT * SEQ, F32R, region + mix_cols * 4)
        attT_lo_t = place("attT_lo", KT * SEQ, F32R, region + mix_cols * 4 + KT * SEQ * 4)
        assert region + mix_cols * 4 + 2 * KT * SEQ * 4 <= nc.sbuf_usable_end

        def tiles(t, k):
            return t[:].rearrange("p (k n) -> p k n", k=k)

        uT_hi, uT_lo = tiles(uT_hi_t, KT), tiles(uT_lo_t, KT)
        hT_hi, hT_lo = tiles(hT_hi_t, HT), tiles(hT_lo_t, HT)
        attT_hi, attT_lo = tiles(attT_hi_t, KT), tiles(attT_lo_t, KT)
        ple_hi, ple_lo = tiles(ple_hi_t, 2), tiles(ple_lo_t, 2)
        pw = tiles(pw_t, TT)
        sg = sg_t[:].rearrange("p (b t n) -> p b t n", b=2, t=TT)
        hs = hs_t[:].rearrange("p (b t n) -> p b t n", b=2, t=TT)

        o = 0
        raw = mix[:, o:o + CT * SEQ].rearrange("p (c n) -> p c n", c=CT)
        o += CT * SEQ
        qT = mix[:, o:o + 2048].rearrange("p (k n) -> p k n", k=8)
        xs = mix[:, o:o + 2048].rearrange("p (t n) -> p t n", t=TT)
        o += 2048
        kdup = mix[:, o:o + 1024].rearrange("p (k n) -> p k n", k=KV)
        xd = mix[:, o:o + 1024]
        o += 1024
        vwin = mix[:, o:o + 2048].rearrange("p (c k u d) -> p c k u d", c=4, k=KV, u=2)
        btok = mix[:, o:o + 256].rearrange("p (g n) -> p g n", g=2)
        cbm = mix[:, o + 256:o + 512].rearrange("p (g n) -> p g n", g=2)
        o += 2048
        zs = mix[:, o:o + 2048].rearrange("p (t n) -> p t n", t=TT)
        o += 2048
        acc = mix[:, o:o + 1024]
        o += 1024
        lg = mix[:, o:o + 1024].rearrange("p (b h j) -> p b h j", b=2, h=4)
        pT = mix[:, o + 1024:o + 2048].rearrange("p (b n) -> p b n", b=2)
        hst = mix[:, o:o + 1024]
        seg = mix[:, o + 1024:o + 2048].rearrange("p (b h l) -> p b h l", b=2, h=4)

        ident = consts[:, K_ID:K_ID + P]
        tri = consts[:, K_TRI:K_TRI + P]
        blk = consts[:, K_BLK:K_BLK + P]

        def small(i):
            return dts[:, 32 * i:32 * i + 32]

        S_DTR, S_V, S_W, S_DT, S_ADT, S_CS, S_ECS, S_EDEC, S_DEC0, S_DEC1 = range(10)

        psA = ctx.enter_context(nc.psum_tensor("psA", [P, 2, 512], F32))
        psB = ctx.enter_context(nc.psum_tensor("psB", [P, 2, 512], F32))
        psC = ctx.enter_context(nc.psum_tensor("psC", [P, 2, 512], F32))
        psD = ctx.enter_context(nc.psum_tensor("psD", [P, 2, 512], F32))
        gemm = [psA, psB]
        turn = [psC, psD]

        setup_in = sem("setup_in")
        params_in_s = sem("params_loaded")
        ple_loaded = sem("ple_loaded")
        row_loaded = [sem(f"row_loaded{s}") for s in range(2)]
        out_stored = sem("out_stored")
        stage_full = [sem(f"stage_full{s}") for s in range(RING)]
        hi_ready = sem("hi_ready")
        lo_ready = sem("lo_ready")
        w_used = sem("w_used")
        gemm_t0 = sem("gemm_t0")
        bias_ps = sem("bias_ps")
        bias_sb = sem("bias_sb")
        silu_ready = sem("silu_ready")
        h_ready = sem("h_ready")
        hT_ps = sem("hT_ps")
        hT_hi_s = sem("hT_hi_ready")
        hT_lo_s = sem("hT_lo_ready")
        ss_ready = sem("ss_ready")
        var_ready = sem("var_ready")
        rstd_ready = sem("rstd_ready")
        norm_mul = sem("norm_mul")
        x_ready = sem("x_ready")
        uT_ps = sem("uT_ps")
        uT_hi_s = sem("uT_hi_ready")
        uT_lo_s = sem("uT_lo_ready")
        ple_hi_s = sem("ple_hi_ready")
        ple_lo_s = sem("ple_lo_ready")
        pw_ready = sem("pw_ready")
        gate_ready = sem("gate_ready")
        gated = sem("gated")
        win_evac = sem("win_evac")
        conv_acc = sem("conv_acc")
        conv_ready = sem("conv_ready")
        score_ps = sem("score_ps")
        logit_ready = sem("logit_ready")
        exp_ready = sem("exp_ready")
        prob_ready = sem("prob_ready")
        pT_ps = sem("pT_ps")
        pT_ready = sem("pT_ready")
        pv_ps = sem("pv_ps")
        att_hi_s = sem("att_hi_ready")
        att_lo_s = sem("att_lo_ready")
        a_ready = sem("a_ready")
        dtv_ready = sem("dtv_ready")
        dexp_ready = sem("dexp_ready")
        adt_ready = sem("adt_ready")
        cs_ps = sem("cs_ps")
        cs_ready = sem("cs_ready")
        dec_ready = sem("dec_ready")
        xT_ps = sem("xT_ps")
        xb_ready = sem("xb_ready")
        cb_ps = sem("cb_ps")
        off_ps = sem("off_ps")
        off_out = sem("off_out")
        st_ps = sem("st_ps")
        st_ready = sem("st_ready")
        seg_ps = sem("seg_ps")
        seg_ready = sem("seg_ready")
        dec_mat = sem("dec_mat")
        m_ready = sem("m_ready")
        diag_ps = sem("diag_ps")
        yg_ready = sem("yg_ready")

        block = ctx.enter_context(nc.Block())

        def att_views(attT, t, kv, par):
            r = slice(HD * par, HD * par + HD)
            dst = attT[r, 2 * kv:2 * kv + 2, t * P:t * P + P].rearrange("p k (f q) -> p k f q", f=2)
            src = psD[r, 1, :].rearrange("p (f u k q) -> p u k f q", f=2, k=2, u=2)[:, par]
            return dst, src

        def stage_value(L, c, i):
            return L * (16 * LOADS) + i * 16 + 16 * (c // RING + 1)

        def chunk_value(L, c, i):
            return L * CHUNKS + i * RING + c + 1

        @block.sync
        def _(sp):
            sp.dma_start(consts[:], consts_in).then_inc(setup_in, 16)
            sp.dma_start(table[0:BUCKETS, :], table_in).then_inc(setup_in, 16)
            sp.dma_start(x_sb, x_in.rearrange("(t p) n -> p t n", p=P)).then_inc(setup_in, 16)
            with sp.Fori(0, DEPTH) as L:
                with sp.Fori(0, LOADS) as i:
                    for s in range(RING):
                        sp.wait_ge(lo_ready, chunk_value(L, s, i))
                        sp.dma_start(stage[s][:], chunks_in[bass.ds((L * CHUNKS + i * RING + s) * P, P), :]) \
                            .then_inc(stage_full[s], 16)
            sp.wait_ge(x_ready, N_X * DEPTH + TT)
            sp.dma_start(out.rearrange("(t p) n -> p t n", p=P), x_sb).then_inc(out_stored, 16)
            sp.wait_ge(out_stored, 16)

        @block.gpsimd
        def _(pool):
            nc.gpsimd.memset(half_neg[:], -0.5)
            pool.drain()

            def load_row(L, r):
                s = ROW_SLOT[r]
                src = rows_in[bass.ds(L * (NORMS + 1) + r, 1), :].broadcast_to([P, D])
                pool.dma_start(rows[s][:], src).then_inc(row_loaded[s], 16)

            def inverse_roots(L, first, n):
                for k in range(first, first + n):
                    b = k % (2 * TT)
                    pool.wait_ge(var_ready, L * N_NORM + k + 1)
                    nc.gpsimd.tensor_tensor(rstd[:, b:b + 1], var[:, b:b + 1], half_neg[:], ALU.pow) \
                        .then_inc(rstd_ready, 1)

            def rows_free(L, n):
                pool.wait_ge(norm_mul, L * N_NORM + n)

            with pool.Fori(0, DEPTH) as L:
                pool.dma_start(params[:], params_in[bass.ds(L * P, P), :]).then_inc(params_in_s, 16)
                load_row(L, 0)
                load_row(L, 1)
                inverse_roots(L, 0, 2)
                rows_free(L, 2)
                load_row(L, 2)
                inverse_roots(L, 2, 4)
                rows_free(L, 6)
                load_row(L, ROW_SSM)
                load_row(L, 3)
                inverse_roots(L, 6, 2)
                rows_free(L, 8)
                load_row(L, 4)
                inverse_roots(L, 8, 4)
                rows_free(L, 12)
                load_row(L, 5)
                load_row(L, 6)
                pool.wait_ge(w_used, L * CHUNKS + C_OUT_SSD + 4 + RING)
                pool.dma_start(ple_raw_t[:].rearrange("p (k n) -> p k n", k=2),
                               ple_in[bass.ds(L * PLE, PLE), :].rearrange("(k p) n -> p k n", p=P)) \
                    .then_inc(ple_loaded, 16)
                inverse_roots(L, 12, 4)
                rows_free(L, 16)
                load_row(L, 7)
                inverse_roots(L, 16, 2)
                rows_free(L, 18)

        @block.tensor
        def _(pe):
            nc.tensor.nop().then_inc(w_used, RING)

            pe.wait_ge(setup_in, 48)
            for j in range(WIN):
                ps = gemm[j // 64][0:CHUNK, (j // 32) % 2, (j % 32) * HEADS:(j % 32 + 1) * HEADS]
                at0 = K_ONEHOT + WIN - 1 - j
                mm = nc.tensor.matmul(ps, consts[0:BUCKETS, at0:at0 + CHUNK], table[0:BUCKETS, :], start=True, stop=True)
            mm.then_inc(bias_ps, 1)

            def chunk_ready(L, c, i=0):
                pe.wait_ge(lo_ready, chunk_value(L, c, i) + RING)

            def three(out_ap, hi, lo, whi, wlo, start, stop, moving_weights=True):
                if moving_weights:
                    nc.tensor.matmul(out_ap, hi, whi, start=start, stop=False, skip_group_check=True)
                    nc.tensor.matmul(out_ap, lo, whi, start=False, stop=False, skip_group_check=True)
                    return nc.tensor.matmul(out_ap, hi, wlo, start=False, stop=stop, skip_group_check=True)
                nc.tensor.matmul(out_ap, whi, hi, start=start, stop=False, skip_group_check=True)
                nc.tensor.matmul(out_ap, whi, lo, start=False, stop=False, skip_group_check=True)
                return nc.tensor.matmul(out_ap, wlo, hi, start=False, stop=stop, skip_group_check=True)

            def wide_half(ps, t, slot, half):
                for k in range(4):
                    kt = 4 * half + k
                    w = slice(512 * k, 512 * k + 512)
                    mm = three(ps, uT_hi[:, kt, t * P:t * P + P], uT_lo[:, kt, t * P:t * P + P],
                               w_hi[slot][:, w], w_lo[slot][:, w], kt == 0, kt == KT - 1)
                return mm

            def transposes(dst, src, n):
                for k in range(n):
                    mm = nc.tensor.transpose(dst[:, k * P:k * P + P], src[:, k * P:k * P + P], ident)
                return mm

            def u_transposes(L, n_mul, n_ut):
                t = n_ut % 2
                pe.wait_ge(norm_mul, L * N_NORM + n_mul + 1)
                ps = turn[t][:].rearrange("p b n -> p (b n)")
                transposes(ps, tm[:, t, :], KT).then_inc(uT_ps, 1)

            def wait_uT(L, n):
                pe.wait_ge(uT_lo_s, L * N_UT + n + 1)

            def ffn_group(L, f, g, c, i):
                ps = gemm[((c - (C_FFN1, C_FFN2)[f]) // 2) % 2]
                for half in range(2):
                    s = (c + half) % RING
                    chunk_ready(L, c + half, i)
                    mm = wide_half(ps[:, 0, :], 0, s, half)
                    if half:
                        mm.then_inc(gemm_t0, 1)
                    wide_half(ps[:, 1, :], 1, s, half).then_inc(w_used, 1)

            def h_transposes(L, f, par, done, g_done):
                pe.wait_ge(h_ready, L * N_H + done)
                ps = turn[par][:, 0, :].rearrange("p (k t n) -> p k t n", k=2, t=TT)
                for t in range(TT):
                    for k in range(2):
                        mm = nc.tensor.transpose(ps[:, k, t, :], hs[:, par, t, k * P:k * P + P], ident)
                mm.then_inc(hT_ps, 1)

            def k_chunk(L, c, t, hi, lo, kt0, last_kt, first):
                s = c % RING
                for k in range(2):
                    for half in range(2):
                        w = slice(k * D + half * 512, k * D + half * 512 + 512)
                        mm = three(first[t][:, half, :], hi[:, kt0 + k, t * P:t * P + P],
                                   lo[:, kt0 + k, t * P:t * P + P], w_hi[s][:, w], w_lo[s][:, w],
                                   (c, k) == first["start"], kt0 + k == last_kt)
                return mm

            def ffn(L, f):
                c0 = (C_FFN1, C_FFN2)[f]
                cd = (C_DOWN1, C_DOWN2)[f]
                hb = f * 2 * GROUPS
                ps = gemm[0]
                wait_uT(L, (0, 6)[f])
                chunk_ready(L, c0)
                wide_half(ps[:, 0, :], 0, c0 % RING, 0)
                chunk_ready(L, c0 + 1)
                wide_half(ps[:, 0, :], 0, (c0 + 1) % RING, 1).then_inc(gemm_t0, 1)
                wait_uT(L, (1, 7)[f])
                wide_half(ps[:, 1, :], 1, c0 % RING, 0).then_inc(w_used, 1)
                wide_half(ps[:, 1, :], 1, (c0 + 1) % RING, 1).then_inc(w_used, 1)
                with pe.Fori(0, (GROUPS - 1) // 2) as i:
                    for par in (1, 0):
                        g0 = 2 - par
                        ffn_group(L, f, None, c0 + 2 * g0, i)
                        h_transposes(L, f, 1 - par, hb + i * 4 + 2 * g0, None)
                out2 = {0: gemm[0], 1: gemm[1], "start": (cd, 0)}
                chunk_ready(L, cd)
                pe.wait_ge(hT_lo_s, L * N_HT + f * GROUPS + GROUPS - 1)
                k_chunk(L, cd, 1, hT_hi, hT_lo, 0, HT - 1, out2)
                h_transposes(L, f, 0, hb + 2 * GROUPS, None)
                k_chunk(L, cd, 0, hT_hi, hT_lo, 0, HT - 1, out2).then_inc(w_used, 1)
                for j in range(1, GROUPS - 2):
                    chunk_ready(L, cd + j)
                    k_chunk(L, cd + j, 0, hT_hi, hT_lo, 2 * j, HT - 1, out2)
                    k_chunk(L, cd + j, 1, hT_hi, hT_lo, 2 * j, HT - 1, out2).then_inc(w_used, 1)
                j = GROUPS - 2
                chunk_ready(L, cd + j)
                k_chunk(L, cd + j, 0, hT_hi, hT_lo, 2 * j, HT - 1, out2)
                chunk_ready(L, cd + j + 1)
                pe.wait_ge(hT_lo_s, L * N_HT + f * GROUPS + GROUPS)
                k_chunk(L, cd + j + 1, 0, hT_hi, hT_lo, 2 * j + 2, HT - 1, out2).then_inc(gemm_t0, 1)
                k_chunk(L, cd + j, 1, hT_hi, hT_lo, 2 * j, HT - 1, out2).then_inc(w_used, 1)
                k_chunk(L, cd + j + 1, 1, hT_hi, hT_lo, 2 * j + 2, HT - 1, out2).then_inc(w_used, 1)

            def win_free(L, k):
                if k >= 2:
                    pe.wait_ge(win_evac, L * N_WIN + k - 1)

            def turned_half(ps, m0, ms, slot, half):
                for m in ms:
                    for k in range(4):
                        w = slice(512 * k + P * m, 512 * k + P * m + P)
                        mm = three(ps[:, (m - m0) // 2, ((m - m0) % 2) * SEQ:((m - m0) % 2 + 1) * SEQ],
                                   uT_hi[:, 4 * half + k, :], uT_lo[:, 4 * half + k, :],
                                   w_hi[slot][:, w], w_lo[slot][:, w],
                                   half == 0 and k == 0 and (m - m0) % 2 == 0,
                                   half == 1 and k == 3, moving_weights=False)
                return mm

            def turned_chunk(L, k, c, half):
                if half == 0:
                    win_free(L, k)
                chunk_ready(L, c + half)
                turned_half(gemm[k % 2], 0, range(4), (c + half) % RING, half).then_inc(w_used, 1)

            def kv_chunk(L, c, half):
                if half == 0:
                    win_free(L, 2)
                chunk_ready(L, c + half)
                s = (c + half) % RING
                turned_half(gemm[0], 0, range(2), s, half)
                for t in range(TT):
                    for k in range(4):
                        kt = 4 * half + k
                        w = slice(512 * k + 256, 512 * k + 512)
                        mm = three(gemm[0][:, 1, 256 * t:256 * t + 256], uT_hi[:, kt, t * P:t * P + P],
                                   uT_lo[:, kt, t * P:t * P + P], w_hi[s][:, w], w_lo[s][:, w],
                                   kt == 0 and t == 0, kt == KT - 1)
                mm.then_inc(w_used, 1)

            def dt_chunk(L):
                win_free(L, 6)
                chunk_ready(L, C_DT)
                s = C_DT % RING
                for t in range(TT):
                    for kt in range(KT):
                        w = slice(16 * kt, 16 * kt + 16)
                        mm = three(gemm[0][:, 0, 16 * t:16 * t + 16], uT_hi[:, kt, t * P:t * P + P],
                                   uT_lo[:, kt, t * P:t * P + P], w_hi[s][:, w], w_lo[s][:, w],
                                   kt == 0 and t == 0, kt == KT - 1)
                mm.then_inc(w_used, 1)

            def z_chunk(L, k, c, half):
                if half == 0:
                    win_free(L, k)
                chunk_ready(L, c + half)
                s = (c + half) % RING
                mm = wide_half(gemm[k % 2][:, 0, :], 0, s, half)
                if half:
                    mm.then_inc(gemm_t0, 1)
                wide_half(gemm[k % 2][:, 1, :], 1, s, half).then_inc(w_used, 1)

            def scores(L, n):
                t, kv = n // KV, n % KV
                for hf in range(2):
                    c = 2 * t + hf
                    lo_tok = max(c - 1, 0) * CHUNK
                    width = (c + 1) * CHUNK - lo_tok
                    for hh in range(4):
                        h = 4 * kv + hh
                        po = HD * (h % 2)
                        mm = nc.tensor.matmul(
                            psC[CHUNK * hf:CHUNK * hf + CHUNK, hh % 2,
                                WIN * (hh // 2) + WIN - width:WIN * (hh // 2) + WIN],
                            qT[po:po + HD, h // 2, c * CHUNK:c * CHUNK + CHUNK],
                            kdup[po:po + HD, kv, lo_tok:lo_tok + width], start=True, stop=True)
                mm.then_inc(score_ps, 1)

            def prob_transposes(L, n):
                pe.wait_ge(prob_ready, L * N_ITEM + n + 1)
                if n >= 1:
                    pe.wait_ge(pT_ready, L * N_ITEM + n)
                transposes(psD[:, 0, :], lg[:, n % 2].rearrange("p h j -> p (h j)"), 4).then_inc(pT_ps, 1)

            def values(L, n):
                t, kv = n // KV, n % KV
                pe.wait_ge(pT_ready, L * N_ITEM + n + 1)
                if n >= 1:
                    pe.wait_ge(att_lo_s, L * N_ITEM + n)
                probs = pT[:, n % 2].rearrange("p (h q) -> p h q", h=4)
                for hf in range(2):
                    v = vwin[:, 2 * t + hf, kv].rearrange("p u d -> p (u d)")
                    mm = nc.tensor.matmul(psD[:, 1, 256 * hf:256 * hf + 256], v,
                                          probs[:, :, hf * CHUNK:hf * CHUNK + CHUNK], start=True, stop=True)
                mm.then_inc(pv_ps, 1)

            def attention_step(L, n):
                if 1 <= n <= N_ITEM:
                    prob_transposes(L, n - 1)
                if 0 <= n < N_ITEM:
                    scores(L, n)
                if 2 <= n <= N_ITEM + 1:
                    values(L, n - 2)

            def decay_sums(L):
                pe.wait_ge(adt_ready, L + 1)
                adt = small(S_ADT)
                nc.tensor.matmul(psC[:, 0, 0:32], tri, adt, start=True, stop=True)
                nc.tensor.matmul(psC[:, 0, 32:64], blk, adt, start=True, stop=True)
                for hf in range(2):
                    ind = consts[:, K_HALF + hf:K_HALF + hf + 1].broadcast_to([P, P])
                    mm = nc.tensor.matmul(psC[:, 0, 64 + 32 * hf:96 + 32 * hf], ind, adt, start=True, stop=True)
                mm.then_inc(cs_ps, 1)

            def ssd_turn(L, t):
                if t == 1:
                    wait_uT(L, 4)
                for k in range(8):
                    nc.tensor.transpose(psC[:, k // 4, (k % 4) * P:(k % 4 + 1) * P],
                                        raw[:, k, t * P:t * P + P], ident)
                for g in range(2):
                    mm = nc.tensor.transpose(psD[:, 0, g * P:g * P + P], raw[:, 8 + g, t * P:t * P + P], ident)
                mm.then_inc(xT_ps, 1)
                for g in range(2):
                    mm = nc.tensor.matmul(psD[:, 1, g * P:g * P + P], raw[:, 8 + g, t * P:t * P + P],
                                          raw[:, 10 + g, t * P:t * P + P], start=True, stop=True)
                mm.then_inc(cb_ps, 1)

            def ssd_off(L, t, hf):
                c = 2 * t + hf
                pe.wait_ge(st_ready, L * 3 + c)
                if hf == 0 or c == 1:
                    pe.wait_ge(xb_ready, L * 4 + 2 * t + 2)
                for g in range(2):
                    mm = nc.tensor.matmul(psD[CHUNK * hf:CHUNK * hf + CHUNK, g, :],
                                          raw[:, 10 + g, c * CHUNK:c * CHUNK + CHUNK],
                                          hst[:, 512 * g:512 * g + 512], start=True, stop=True)
                mm.then_inc(off_ps, 1)

            def ssd_state(L, t, hf):
                c = 2 * t + hf
                if hf == 0:
                    pe.wait_ge(xb_ready, L * 4 + 2 * t + 2)
                else:
                    pe.wait_ge(st_ready, L * 3 + c)
                rows_ = slice(CHUNK * hf, CHUNK * hf + CHUNK)
                for g in range(2):
                    mm = nc.tensor.matmul(psC[:, g, :], btok[rows_, g, :], xd[rows_, 512 * g:512 * g + 512],
                                          start=True, stop=True)
                mm.then_inc(st_ps, 1)

            def seg_sums(L, t, q):
                if q == 0:
                    pe.wait_ge(off_out, L * 2 + t + 1)
                if q >= 2:
                    pe.wait_ge(seg_ready, L * 8 + 4 * t + q - 1)
                for hh in range(4):
                    h = 16 * t + 4 * q + hh
                    mm = nc.tensor.matmul(psD[:, q % 2, hh * P:hh * P + P],
                                          small(S_ADT)[:, h:h + 1].broadcast_to([P, P]), tri,
                                          start=True, stop=True)
                mm.then_inc(seg_ps, 1)

            def diag(L, t, q):
                pe.wait_ge(m_ready, L * 8 + 4 * t + q + 1)
                if t == 0 and q == 0:
                    pe.wait_ge(st_ready, L * 3 + 2)
                if t == 1 and q == 0:
                    pe.wait_ge(st_ready, L * 3 + 3)
                for hh in range(4):
                    h = 4 * q + hh
                    mm = nc.tensor.matmul(psC[:, h // 8, (h % 8) * HD:(h % 8 + 1) * HD], seg[:, q % 2, hh, :],
                                          tm[:, t, h * HD:h * HD + HD], start=True, stop=True)
                mm.then_inc(diag_ps, 1)

            def ssd(L, t):
                ssd_turn(L, t)
                for hf in range(2):
                    if 2 * t + hf >= 1:
                        ssd_off(L, t, hf)
                    if 2 * t + hf < 3:
                        ssd_state(L, t, hf)
                for q in range(4):
                    seg_sums(L, t, q)
                    if q >= 1:
                        diag(L, t, q - 1)
                diag(L, t, 3)
                u_transposes(L, 6 + t, 4 + t)

            pe.wait_ge(bias_sb, 1)
            with pe.Fori(0, DEPTH) as L:
                u_transposes(L, 0, 0)
                u_transposes(L, 1, 1)
                ffn(L, 0)
                u_transposes(L, 3, 2)
                u_transposes(L, 5, 3)
                wait_uT(L, 2)
                wait_uT(L, 3)
                for k in range(2):
                    for half in range(2):
                        turned_chunk(L, k, C_Q + 2 * k, half)
                for half in range(2):
                    kv_chunk(L, C_KV, half)
                step = -1
                for k in range(3):
                    for half in range(2):
                        if step == 0:
                            pe.wait_ge(win_evac, L * N_WIN + 3)
                        turned_chunk(L, 3 + k, C_XBC + 2 * k, half)
                        attention_step(L, step)
                        step += 1
                dt_chunk(L)
                attention_step(L, step)
                step += 1
                for k in range(2):
                    for half in range(2):
                        z_chunk(L, 7 + k, C_Z + 2 * k, half)
                        attention_step(L, step)
                        step += 1
                pe.wait_ge(att_lo_s, L * N_ITEM + N_ITEM)
                decay_sums(L)
                out2 = {0: gemm[0], 1: gemm[1], "start": (C_OUT_ATT, 0)}
                pe.wait_ge(win_evac, L * N_WIN + N_WIN)
                pe.wait_ge(conv_ready, L * 3 + 3)
                pe.wait_ge(dec_ready, L + 1)
                for j in range(4):
                    c = C_OUT_ATT + j
                    chunk_ready(L, c)
                    k_chunk(L, c, 1, attT_hi, attT_lo, 2 * j, -1, out2)
                    k_chunk(L, c, 0, attT_hi, attT_lo, 2 * j, -1, out2).then_inc(w_used, 1)
                for t in range(TT):
                    ssd(L, t)
                wait_uT(L, 4)
                wait_uT(L, 5)
                for j in range(2):
                    c = C_OUT_SSD + j
                    chunk_ready(L, c)
                    k_chunk(L, c, 0, uT_hi, uT_lo, 2 * j, KT - 1, out2)
                    k_chunk(L, c, 1, uT_hi, uT_lo, 2 * j, KT - 1, out2).then_inc(w_used, 1)
                c = C_OUT_SSD + 2
                chunk_ready(L, c)
                k_chunk(L, c, 0, uT_hi, uT_lo, 4, KT - 1, out2)
                chunk_ready(L, c + 1)
                k_chunk(L, c + 1, 0, uT_hi, uT_lo, 6, KT - 1, out2).then_inc(gemm_t0, 1)
                k_chunk(L, c, 1, uT_hi, uT_lo, 4, KT - 1, out2).then_inc(w_used, 1)
                k_chunk(L, c + 1, 1, uT_hi, uT_lo, 6, KT - 1, out2).then_inc(w_used, 1)
                u_transposes(L, 9, 6)
                u_transposes(L, 11, 7)
                ffn(L, 1)
                chunk_ready(L, C_PLE)
                pe.wait_ge(ple_lo_s, L + 1)
                outp = {0: psC, 1: psD, "start": (C_PLE, 0)}
                k_chunk(L, C_PLE, 0, ple_hi, ple_lo, 0, 1, outp).then_inc(gemm_t0, 1)
                k_chunk(L, C_PLE, 1, ple_hi, ple_lo, 0, 1, outp).then_inc(w_used, 1)
                pe.wait_ge(pw_ready, L * 2 + 1)
                u_transposes(L, 13, 8)
                pe.wait_ge(pw_ready, L * 2 + 2)
                u_transposes(L, 15, 9)
                outg = {0: gemm[0], 1: gemm[1], "start": (C_GATE, 0)}
                wait_uT(L, 8)
                chunk_ready(L, C_GATE)
                k_chunk(L, C_GATE, 0, uT_hi, uT_lo, 0, KT - 1, outg)
                chunk_ready(L, C_GATE + 1)
                k_chunk(L, C_GATE + 1, 0, uT_hi, uT_lo, 2, KT - 1, outg)
                wait_uT(L, 9)
                k_chunk(L, C_GATE, 1, uT_hi, uT_lo, 0, KT - 1, outg).then_inc(w_used, 1)
                k_chunk(L, C_GATE + 1, 1, uT_hi, uT_lo, 2, KT - 1, outg).then_inc(w_used, 1)
                c = C_GATE + 2
                chunk_ready(L, c)
                k_chunk(L, c, 0, uT_hi, uT_lo, 4, KT - 1, outg)
                chunk_ready(L, c + 1)
                k_chunk(L, c + 1, 0, uT_hi, uT_lo, 6, KT - 1, outg).then_inc(gemm_t0, 1)
                k_chunk(L, c, 1, uT_hi, uT_lo, 4, KT - 1, outg).then_inc(w_used, 1)
                k_chunk(L, c + 1, 1, uT_hi, uT_lo, 6, KT - 1, outg).then_inc(w_used, 1)

        @block.scalar
        def _(act):
            def copy(dst, src):
                return nc.scalar.activation(dst, src, ACT.Copy)

            act.wait_ge(bias_ps, 1)
            for b in range(4):
                for u in range(2):
                    for par in range(2):
                        src = gemm[b // 2][0:CHUNK, b % 2, :].rearrange("p (j v k u) -> p u v k j", v=KV, k=2, u=2)
                        dst = bias[CHUNK * u:CHUNK * u + CHUNK, :, 32 * b:32 * b + 32] \
                            .rearrange("p (v u k) j -> p u v k j", v=KV, u=2)
                        last = copy(dst[:, par], src[:, par])
            last.then_inc(bias_sb, 1)

            def split(L, c, i=0):
                s = c % RING
                act.wait_ge(stage_full[s], stage_value(L, c, i))
                act.wait_ge(w_used, chunk_value(L, c, i))
                copy(w_hi[s][:], stage[s][:]).then_inc(hi_ready, 1)

            def tok0(L, n, i=0):
                act.wait_ge(gemm_t0, L * N_T0 + i + n + 1)

            def tok1(L, c, i=0):
                act.wait_ge(w_used, chunk_value(L, c, i) + RING)

            def square(L, n, src):
                t = {16: 0, 17: 1}.get(n, None)
                b = n % (2 * TT)
                nc.scalar.activation(tm[:, NORM_TILE[n], :], src, ACT.Square,
                                     accum_out=ss[:, b:b + 1]).then_inc(ss_ready, 1)

            def y_flat(t):
                return gemm[t][:].rearrange("p b n -> p (b n)")

            def u_hi(L, n):
                t = n % 2
                act.wait_ge(uT_ps, L * N_UT + n + 1)
                copy(uT_hi[:, :, t * P:t * P + P],
                     turn[t][:].rearrange("p b (k n) -> p (b k) n", n=P)).then_inc(uT_hi_s, 1)

            def x_square(L, n, nx, t):
                act.wait_ge(x_ready, L * N_X + nx + 1)
                square(L, n, x_sb[:, t, :])

            def boundary(L, n0, t0_at, c_last, nx, nu, between=None):
                tok0(L, t0_at)
                square(L, n0, y_flat(0))
                x_square(L, n0 + 1, nx, 0)
                tok1(L, c_last)
                square(L, n0 + 2, y_flat(1))
                if between:
                    between()
                u_hi(L, nu)
                x_square(L, n0 + 3, nx + 1, 1)
                u_hi(L, nu + 1)

            def ffn_gates(L, f, par, g0, i, c):
                for t in range(TT):
                    if t == 0:
                        tok0(L, T0_FFN[f] + g0, 0 if isinstance(i, int) and i == 0 else i * 2)
                    else:
                        tok1(L, c + 1, i)
                    nc.scalar.activation(sg[:, par, t, :], gemm[par][:, t, 0:FW], ACT.Silu) \
                        .then_inc(silu_ready, 1)

            def h_hi(L, f, par, g0, i):
                act.wait_ge(hT_ps, L * N_HT + f * GROUPS + g0 + i * 2 + 1)
                dst = hT_hi_t[:, bass.ds(i * 4 * SEQ + g0 * 2 * SEQ, 2 * SEQ)] if not isinstance(i, int) \
                    else hT_hi_t[:, g0 * 2 * SEQ:(g0 + 1) * 2 * SEQ]
                copy(dst, turn[par][:, 0, :]).then_inc(hT_hi_s, 1)

            def ffn(L, f):
                c0, cd = (C_FFN1, C_FFN2)[f], (C_DOWN1, C_DOWN2)[f]
                split(L, c0 + 3)
                split(L, c0 + 4)
                ffn_gates(L, f, 0, 0, 0, c0)
                with act.Fori(0, (GROUPS - 1) // 2) as i:
                    for par in (1, 0):
                        g0 = 2 - par
                        split(L, c0 + 2 * g0 + 3, i)
                        split(L, c0 + 2 * g0 + 4, i)
                        ffn_gates(L, f, par, g0, i, c0 + 2 * g0)
                        h_hi(L, f, 1 - par, g0 - 1, i)
                split(L, cd + 3)
                h_hi(L, f, 0, GROUPS - 1, 0)
                for j in range(1, GROUPS - 1):
                    split(L, cd + j + 3)

            def attention_step(L, n):
                if 0 <= n < N_ITEM:
                    b = n % 2
                    sm = att_s[:, 20 * b:20 * b + 20]
                    act.wait_ge(logit_ready, L * N_ITEM + n + 1)
                    for hh in range(4):
                        nc.scalar.activation(lg[:, b, hh, :], lg[:, b, hh, :], ACT.Exp,
                                             bias=sm[:, 4 + hh:5 + hh], accum_out=sm[:, 12 + hh:13 + hh])
                    nc.scalar.activation(sm[:, 8:12], sm[:, 8:12], ACT.Exp).then_inc(exp_ready, 1)
                if 1 <= n <= N_ITEM:
                    act.wait_ge(pT_ps, L * N_ITEM + n)
                    if n >= 3:
                        act.wait_ge(pv_ps, L * N_ITEM + n - 2)
                    copy(pT[:, (n - 1) % 2], psD[:, 0, :]).then_inc(pT_ready, 1)
                if 2 <= n <= N_ITEM + 1:
                    m = n - 2
                    t, kv = m // KV, m % KV
                    act.wait_ge(pv_ps, L * N_ITEM + m + 1)
                    for par in range(2):
                        dst, src = att_views(attT_hi, t, kv, par)
                        last = copy(dst, src)
                    last.then_inc(att_hi_s, 1)

            def group_evac(L, k):
                ps = gemm[k % 2]
                if k < 2:
                    last = copy(qT[:, 4 * k:4 * k + 4, :], ps[:].rearrange("p b (m n) -> p (b m) n", n=SEQ))
                elif k == 2:
                    for kv in range(KV):
                        src = ps[HD * (kv % 2):HD * (kv % 2) + HD, 0, SEQ * (kv // 2):SEQ * (kv // 2) + SEQ]
                        for u in range(2):
                            copy(kdup[HD * u:HD * u + HD, kv, :], src)
                    top, low, every = slice(0, CHUNK), slice(CHUNK, P), slice(0, P)
                    for to, w, of, t in ((every, 1, every, 0), (every, 3, every, 1), (low, 0, top, 0),
                                         (top, 2, low, 0), (low, 2, top, 1)):
                        v = ps[of, 1, 256 * t:256 * t + 256].rearrange("p (k u d) -> p k u d", k=KV, u=1)
                        last = copy(vwin[to, w], v.broadcast_to([v.shape[0], KV, 2, HD]))
                elif k < 6:
                    last = copy(raw[:, 4 * (k - 3):4 * (k - 3) + 4, :],
                                ps[:].rearrange("p b (m n) -> p (b m) n", n=SEQ))
                elif k == 6:
                    last = copy(small(S_DTR), ps[:, 0, 0:32])
                last.then_inc(win_evac, 1)

            def conv_silu(L, b):
                act.wait_ge(conv_acc, L * 3 + b + 1)
                nc.scalar.activation(raw[:, 4 * b:4 * b + 4, :],
                                     acc.rearrange("p (c n) -> p c n", c=4), ACT.Silu).then_inc(conv_ready, 1)

            def ssd(L, t):
                for q in range(4):
                    act.wait_ge(seg_ready, L * 8 + 4 * t + q + 1)
                    nc.scalar.activation(seg[:, q % 2], seg[:, q % 2], ACT.Exp).then_inc(dec_mat, 1)
                act.wait_ge(yg_ready, L * 2 + t + 1)
                square(L, 6 + t, xs[:, t, :])
                u_hi(L, 4 + t)

            with act.Fori(0, DEPTH) as L:
                for c in range(AHEAD):
                    split(L, c)
                x_square(L, 0, 0, 0)
                x_square(L, 1, 1, 1)
                u_hi(L, 0)
                u_hi(L, 1)
                act.wait_ge(params_in_s, L * 16 + 16)
                nc.scalar.activation(soft[:], params[:, A_ALOG:A_ALOG + HEADS], ACT.Exp).then_inc(a_ready, 1)
                ffn(L, 0)
                boundary(L, 2, T0_DOWN[0], C_DOWN1 + GROUPS - 1, 2, 2)
                split(L, C_DOWN1 + GROUPS - 1 + 3)
                for k in range(3):
                    for half in range(2):
                        split(L, C_Q + 2 * k + half + 3)
                    tok1(L, C_Q + 2 * k + 1)
                    group_evac(L, k)
                step = -1
                for k in range(3):
                    for half in range(2):
                        split(L, C_XBC + 2 * k + half + 3)
                        if half == 0 and k >= 1:
                            conv_silu(L, k - 1)
                        if half == 1:
                            tok1(L, C_XBC + 2 * k + 1)
                            group_evac(L, 3 + k)
                        attention_step(L, step)
                        step += 1
                split(L, C_DT + 3)
                tok1(L, C_DT)
                group_evac(L, 6)
                conv_silu(L, 2)
                attention_step(L, step)
                step += 1
                for k in range(2):
                    for half in range(2):
                        split(L, C_Z + 2 * k + half + 3)
                        if half == 1:
                            tok0(L, T0_Z + k)
                            for t in range(TT):
                                if t == 1:
                                    tok1(L, C_Z + 2 * k + 1)
                                last = nc.scalar.activation(zs[:, t, 512 * k:512 * k + 512],
                                                            gemm[(7 + k) % 2][:, t, :], ACT.Silu)
                            last.then_inc(win_evac, 1)
                        if step == N_ITEM - 1:
                            act.wait_ge(dtv_ready, L + 1)
                            nc.scalar.activation(small(S_W), small(S_W), ACT.Exp).then_inc(dexp_ready, 1)
                        attention_step(L, step)
                        step += 1
                act.wait_ge(cs_ready, L + 1)
                nc.scalar.activation(dts[:, 32 * S_ECS:32 * (S_DEC1 + 1)], dts[:, 32 * S_ECS:32 * (S_DEC1 + 1)],
                                     ACT.Exp).then_inc(dec_ready, 1)
                for j in range(4):
                    split(L, C_OUT_ATT + j + 3)
                ssd(L, 0)
                ssd(L, 1)
                for j in range(3):
                    split(L, C_OUT_SSD + j + 3)
                boundary(L, 8, T0_OUT, C_OUT_SSD + 3, 4, 6)
                split(L, C_OUT_SSD + 3 + 3)
                act.wait_ge(ple_loaded, L * 16 + 16)
                copy(ple_hi_t[:], ple_raw_t[:]).then_inc(ple_hi_s, 1)
                ffn(L, 1)

                def pw_out():
                    tok0(L, T0_PLE)
                    copy(pw[:, 0, :], psC[:].rearrange("p b n -> p (b n)")).then_inc(pw_ready, 1)
                    tok1(L, C_PLE)
                    copy(pw[:, 1, :], psD[:].rearrange("p b n -> p (b n)")).then_inc(pw_ready, 1)

                boundary(L, 12, T0_DOWN[1], C_DOWN2 + GROUPS - 1, 6, 8, pw_out)
                split(L, C_PLE + 2)
                split(L, C_PLE + 3)
                split(L, C_GATE + 3)
                for t in range(TT):
                    if t == 0:
                        tok0(L, T0_GATE)
                    else:
                        tok1(L, C_GATE + 3)
                    nc.scalar.activation(tm[:, t, :], y_flat(t), ACT.Sigmoid).then_inc(gate_ready, 1)
                for t in range(TT):
                    act.wait_ge(gated, L * 2 + t + 1)
                    square(L, 16 + t, pw[:, t, :])

        @block.vector
        def _(dve):
            nc.vector.nop().then_inc(lo_ready, RING)

            def split(L, c, i=0):
                s = c % RING
                dve.wait_ge(hi_ready, chunk_value(L, c, i))
                nc.vector.tensor_tensor(w_lo[s][:], stage[s][:], w_hi[s][:].bitcast(F32), ALU.subtract) \
                    .then_inc(lo_ready, 1)

            def fence():
                dve.drain()

            def variance(L, n):
                b = n % (2 * TT)
                dve.wait_ge(ss_ready, L * N_NORM + n + 1)
                nc.vector.tensor_scalar(var[:, b:b + 1], ss[:, b:b + 1], 1.0 / D, EPS, ALU.mult, ALU.add) \
                    .then_inc(var_ready, 1)

            def norm_row(L, n, r, dst, src):
                b = n % (2 * TT)
                dve.wait_ge(rstd_ready, L * N_NORM + n + 1)
                s = ROW_SLOT[r]
                dve.wait_ge(row_loaded[s], L * (16 * ROW_LOADS[s]) + 16 * ROW_NTH[r])
                nc.vector.scalar_tensor_tensor(dst, src, rstd[:, b:b + 1], rows[s][:], ALU.mult, ALU.mult) \
                    .then_inc(norm_mul, 1)

            def y_flat(t):
                return gemm[t][:].rearrange("p b n -> p (b n)")

            def post(L, n, r, t, src, step):
                variance(L, n)
                norm_row(L, n, r, tm[:, t, :], src)
                fence()
                nc.vector.scalar_tensor_tensor(x_sb[:, t, :], tm[:, t, :], step, x_sb[:, t, :],
                                               ALU.mult, ALU.add).then_inc(x_ready, 1)

            def pre(L, n, r, t):
                variance(L, n)
                norm_row(L, n, r, tm[:, t, :], x_sb[:, t, :])

            def u_lo(L, n):
                t = n % 2
                dve.wait_ge(uT_hi_s, L * N_UT + n + 1)
                nc.vector.tensor_tensor(uT_lo[:, :, t * P:t * P + P],
                                        turn[t][:].rearrange("p b (k n) -> p (b k) n", n=P),
                                        uT_hi[:, :, t * P:t * P + P].bitcast(F32),
                                        ALU.subtract).then_inc(uT_lo_s, 1)

            def boundary(L, n0, r_post, r_pre, step, nu):
                post(L, n0, r_post, 0, y_flat(0), step)
                pre(L, n0 + 1, r_pre, 0)
                post(L, n0 + 2, r_post, 1, y_flat(1), step)
                u_lo(L, nu)
                pre(L, n0 + 3, r_pre, 1)
                u_lo(L, nu + 1)

            def products(L, f, par, g0, i):
                for t in range(TT):
                    dve.wait_ge(silu_ready, L * N_H + f * 2 * GROUPS + 2 * g0 + i * 4 + t + 1)
                    nc.vector.tensor_tensor(hs[:, par, t, :], gemm[par][:, t, FW:2 * FW], sg[:, par, t, :],
                                            ALU.mult).then_inc(h_ready, 1)

            def h_lo(L, f, par, g0, i):
                dve.wait_ge(hT_hi_s, L * N_HT + f * GROUPS + g0 + i * 2 + 1)
                at_ = bass.ds(i * 4 * SEQ + g0 * 2 * SEQ, 2 * SEQ) if not isinstance(i, int) \
                    else slice(g0 * 2 * SEQ, (g0 + 1) * 2 * SEQ)
                nc.vector.tensor_tensor(hT_lo_t[:, at_], turn[par][:, 0, :], hT_hi_t[:, at_].bitcast(F32),
                                        ALU.subtract).then_inc(hT_lo_s, 1)

            def ffn(L, f):
                c0, cd = (C_FFN1, C_FFN2)[f], (C_DOWN1, C_DOWN2)[f]
                split(L, c0 + 3)
                split(L, c0 + 4)
                products(L, f, 0, 0, 0)
                with dve.Fori(0, (GROUPS - 1) // 2) as i:
                    for par in (1, 0):
                        g0 = 2 - par
                        split(L, c0 + 2 * g0 + 3, i)
                        split(L, c0 + 2 * g0 + 4, i)
                        products(L, f, par, g0, i)
                        h_lo(L, f, 1 - par, g0 - 1, i)
                split(L, cd + 3)
                h_lo(L, f, 0, GROUPS - 1, 0)
                for j in range(1, GROUPS - 1):
                    split(L, cd + j + 3)

            def attention_step(L, n):
                if 0 <= n < N_ITEM:
                    t, kv = n // KV, n % KV
                    b = n % 2
                    sm = att_s[:, 20 * b:20 * b + 20]
                    bs = bias[:, 4 * kv:4 * kv + 4, :].rearrange("p (u k) j -> p u (k j)", u=2)
                    lgu = lg[:, b].rearrange("p (u k) j -> p u (k j)", u=2)
                    sc = psC[:, :, 0:2 * WIN]
                    dve.wait_ge(score_ps, L * N_ITEM + n + 1)
                    if n >= 2:
                        dve.wait_ge(pT_ps, L * N_ITEM + n - 1)
                    if t == 0:
                        nc.vector.memset(lg[0:CHUNK, b, :, 0:CHUNK], MASKED)
                        for u in range(2):
                            nc.vector.scalar_tensor_tensor(
                                lg[0:CHUNK, b, 2 * u:2 * u + 2, CHUNK:],
                                psC[0:CHUNK, u, 0:2 * WIN].rearrange("p (k j) -> p k j", k=2)[:, :, CHUNK:], SCALE,
                                bias[0:CHUNK, 4 * kv + 2 * u:4 * kv + 2 * u + 2, CHUNK:], ALU.mult, ALU.add)
                        nc.vector.scalar_tensor_tensor(lgu[CHUNK:], sc[CHUNK:], SCALE, bs[CHUNK:],
                                                       ALU.mult, ALU.add)
                    else:
                        nc.vector.scalar_tensor_tensor(lgu, sc, SCALE, bs, ALU.mult, ALU.add)
                    fence()
                    sink = params[:, A_SINK + 4 * kv:A_SINK + 4 * kv + 4]
                    nc.vector.tensor_reduce(sm[:, 0:4], lg[:, b], AX, ALU.max)
                    fence()
                    nc.vector.tensor_tensor(sm[:, 0:4], sm[:, 0:4], sink, ALU.max)
                    fence()
                    nc.vector.tensor_scalar(sm[:, 4:8], sm[:, 0:4], -1.0, None, ALU.mult)
                    nc.vector.tensor_tensor(sm[:, 8:12], sink, sm[:, 0:4], ALU.subtract).then_inc(logit_ready, 1)
                    dve.wait_ge(exp_ready, L * N_ITEM + n + 1)
                    nc.vector.tensor_tensor(sm[:, 12:16], sm[:, 12:16], sm[:, 8:12], ALU.add)
                    fence()
                    nc.vector.reciprocal(sm[:, 16:20], sm[:, 12:16])
                    fence()
                    nc.vector.tensor_tensor(lg[:, b], lg[:, b],
                                            sm[:, 16:20].rearrange("p (h u) -> p h u", u=1)
                                            .broadcast_to([P, 4, WIN]), ALU.mult).then_inc(prob_ready, 1)
                if 2 <= n <= N_ITEM + 1:
                    m = n - 2
                    t, kv = m // KV, m % KV
                    dve.wait_ge(att_hi_s, L * N_ITEM + m + 1)
                    for par in range(2):
                        dst, src = att_views(attT_lo, t, kv, par)
                        hi, _ = att_views(attT_hi, t, kv, par)
                        last = nc.vector.tensor_tensor(dst, src, hi.bitcast(F32), ALU.subtract)
                    last.then_inc(att_lo_s, 1)

            def conv(L, b):
                dve.wait_ge(win_evac, L * N_WIN + 4 + b)
                if b:
                    dve.wait_ge(conv_ready, L * 3 + b)
                a = acc.rearrange("p (c n) -> p c n", c=4)
                for k in range(4):
                    ct = 4 * b + k
                    nc.vector.tensor_scalar(a[:, k, :], raw[:, ct, :],
                                            params[:, A_CW + 4 * ct + 3:A_CW + 4 * ct + 4],
                                            params[:, A_CB + ct:A_CB + ct + 1], ALU.mult, ALU.add)
                for tap in (2, 1, 0):
                    fence()
                    d = CONVW - 1 - tap
                    for k in range(4):
                        ct = 4 * b + k
                        w = params[:, A_CW + 4 * ct + tap:A_CW + 4 * ct + tap + 1]
                        last = nc.vector.scalar_tensor_tensor(a[:, k, d:], raw[:, ct, :SEQ - d], w, a[:, k, d:],
                                                              ALU.mult, ALU.add)
                last.then_inc(conv_acc, 1)

            def over_heads(ap16, n=HD):
                return ap16.rearrange("p (h u) -> p h u", u=1).broadcast_to([P, ap16.shape[1], n])

            def dt_front(L):
                dve.wait_ge(win_evac, L * N_WIN + 7)
                r2 = small(S_DTR).rearrange("p (t h) -> p t h", t=TT)
                v2 = small(S_V).rearrange("p (t h) -> p t h", t=TT)
                for t in range(TT):
                    nc.vector.tensor_tensor(v2[:, t, :], r2[:, t, :], params[:, A_DTB:A_DTB + HEADS], ALU.add)
                fence()
                nc.vector.tensor_scalar(small(S_W), small(S_V), -1.0, None, ALU.mult)
                fence()
                nc.vector.tensor_tensor(small(S_W), small(S_W), small(S_V), ALU.min).then_inc(dtv_ready, 1)

            def dt_back(L):
                dve.wait_ge(dexp_ready, L + 1)
                e, den, r, s2, p_ = (small(S_W), small(S_CS), small(S_DTR), small(S_ECS), small(S_EDEC))
                nc.vector.tensor_scalar(den, e, 2.0, None, ALU.add)
                fence()
                nc.vector.reciprocal(r, den)
                fence()
                nc.vector.tensor_tensor(r, r, e, ALU.mult)
                fence()
                nc.vector.tensor_tensor(s2, r, r, ALU.mult)
                fence()
                nc.vector.tensor_scalar(p_, s2, 2.0 / 15, 2.0 / 13, ALU.mult, ALU.add)
                for n in (11, 9, 7, 5, 3, 1):
                    fence()
                    nc.vector.tensor_tensor(p_, p_, s2, ALU.mult)
                    fence()
                    nc.vector.tensor_scalar(p_, p_, 2.0 / n, None, ALU.add)
                fence()
                nc.vector.tensor_tensor(p_, p_, r, ALU.mult)
                fence()
                nc.vector.scalar_tensor_tensor(small(S_DT), small(S_V), 0.0, p_, ALU.max, ALU.add)
                fence()
                dve.wait_ge(a_ready, L + 1)
                for t in range(TT):
                    sl = slice(32 * S_DT + 16 * t, 32 * S_DT + 16 * t + 16)
                    so = slice(32 * S_ADT + 16 * t, 32 * S_ADT + 16 * t + 16)
                    last = nc.vector.scalar_tensor_tensor(dts[:, so], dts[:, sl], -1.0, soft[:],
                                                          ALU.mult, ALU.mult)
                last.then_inc(adt_ready, 1)

            def decays(L):
                dve.wait_ge(cs_ps, L + 1)
                nc.vector.tensor_copy(small(S_CS), psC[:, 0, 0:32])
                nc.vector.tensor_copy(small(S_ECS), psC[:, 0, 0:32])
                nc.vector.tensor_copy(dts[:, 32 * S_DEC0:32 * S_DEC0 + 64], psC[:, 0, 64:128])
                fence()
                nc.vector.tensor_tensor(small(S_EDEC), psC[:, 0, 32:64], small(S_CS), ALU.subtract) \
                    .then_inc(cs_ready, 1)

            def heads(ap):
                return ap.rearrange("p (h d) -> p h d", d=HD)

            def half_of(i, t):
                return dts[:, 32 * i + 16 * t:32 * i + 16 * t + 16]

            def ssd(L, t):
                dve.wait_ge(xT_ps, L * 2 + t + 1)
                if t == 0:
                    dve.wait_ge(dec_ready, L + 1)
                xps = psC[:].rearrange("p b n -> p (b n)")
                nc.vector.tensor_tensor(heads(tm[:, t, :]), heads(xps), over_heads(half_of(S_DT, t)), ALU.mult)
                nc.vector.tensor_tensor(heads(xs[:, t, :]), heads(xps),
                                        over_heads(params[:, A_DSKIP:A_DSKIP + HEADS]), ALU.mult)
                nc.vector.tensor_copy(btok, psD[:, 0, 0:256].rearrange("p (g n) -> p g n", g=2))
                fence()
                nc.vector.tensor_tensor(heads(xd), heads(tm[:, t, :]), over_heads(half_of(S_EDEC, t)), ALU.mult) \
                    .then_inc(xb_ready, 1)
                dve.wait_ge(cb_ps, L * 2 + t + 1)
                nc.vector.tensor_tensor(cbm, psD[:, 1, 0:256].rearrange("p (g n) -> p g n", g=2),
                                        tri.rearrange("p (u n) -> p u n", u=1).broadcast_to([P, 2, P]),
                                        ALU.mult).then_inc(xb_ready, 1)
                for hf in range(2):
                    c = 2 * t + hf
                    if c >= 1:
                        r = slice(CHUNK * hf, CHUNK * hf + CHUNK)
                        dve.wait_ge(off_ps, L * 3 + c)
                        last = nc.vector.tensor_tensor(
                            heads(acc)[r], heads(psD[:].rearrange("p b n -> p (b n)"))[r],
                            over_heads(half_of(S_ECS, t))[r], ALU.mult)
                        if hf:
                            last.then_inc(off_out, 1)
                    if c < 3:
                        dve.wait_ge(st_ps, L * 3 + c + 1)
                        sps = psC[:].rearrange("p b n -> p (b n)")
                        if c == 0:
                            nc.vector.tensor_copy(hst, sps).then_inc(st_ready, 1)
                        else:
                            nc.vector.tensor_tensor(heads(hst), heads(hst),
                                                    over_heads(half_of(S_DEC0 + hf, t)), ALU.mult)
                            fence()
                            nc.vector.tensor_tensor(hst, hst, sps, ALU.add).then_inc(st_ready, 1)
                fence()
                r = slice(CHUNK if t == 0 else 0, P)
                nc.vector.tensor_tensor(xs[r, t, :], xs[r, t, :], acc[r, :], ALU.add)
                for q in range(4):
                    b = q % 2
                    dve.wait_ge(seg_ps, L * 8 + 4 * t + q + 1)
                    if q >= 2 or t >= 1:
                        dve.wait_ge(diag_ps, L * 8 + 4 * t + q - 1)
                    cs4 = dts[:, 32 * S_CS + 16 * t + 4 * q:32 * S_CS + 16 * t + 4 * q + 4]
                    nc.vector.tensor_tensor(seg[:, b], psD[:, b, :].rearrange("p (h l) -> p h l", h=4),
                                            over_heads(cs4, P), ALU.subtract)
                    fence()
                    nc.vector.tensor_scalar(seg[:, b], seg[:, b], 0.0, None, ALU.min).then_inc(seg_ready, 1)
                    dve.wait_ge(dec_mat, L * 8 + 4 * t + q + 1)
                    nc.vector.tensor_tensor(seg[:, b], seg[:, b],
                                            cbm[:, q // 2, :].rearrange("p (u l) -> p u l", u=1)
                                            .broadcast_to([P, 4, P]), ALU.mult).then_inc(m_ready, 1)
                dve.wait_ge(diag_ps, L * 8 + 4 * t + 4)
                nc.vector.tensor_tensor(xs[:, t, :], psC[:].rearrange("p b n -> p (b n)"), xs[:, t, :], ALU.add)
                fence()
                nc.vector.tensor_tensor(xs[:, t, :], xs[:, t, :], zs[:, t, :], ALU.mult).then_inc(yg_ready, 1)
                variance(L, 6 + t)
                norm_row(L, 6 + t, ROW_SSM, tm[:, t, :], xs[:, t, :])
                u_lo(L, 4 + t)

            dve.wait_ge(setup_in, 48)
            nc.vector.nop().then_inc(x_ready, TT)
            with dve.Fori(0, DEPTH) as L:
                for c in range(AHEAD):
                    split(L, c)
                pre(L, 0, 0, 0)
                pre(L, 1, 0, 1)
                u_lo(L, 0)
                u_lo(L, 1)
                ffn(L, 0)
                boundary(L, 2, 1, 2, 0.5, 2)
                split(L, C_DOWN1 + GROUPS - 1 + 3)
                dve.wait_ge(params_in_s, L * 16 + 16)
                nc.vector.memset(vwin[0:CHUNK, 0], 0.0)
                for c in range(6):
                    split(L, C_Q + c + 3)
                step = -1
                for k in range(3):
                    for half in range(2):
                        split(L, C_XBC + 2 * k + half + 3)
                        if half == 0 and k >= 1:
                            conv(L, k - 1)
                        attention_step(L, step)
                        step += 1
                split(L, C_DT + 3)
                conv(L, 2)
                attention_step(L, step)
                step += 1
                for k in range(2):
                    for half in range(2):
                        split(L, C_Z + 2 * k + half + 3)
                        if step == N_ITEM - 2:
                            dt_front(L)
                        if step == N_ITEM:
                            dt_back(L)
                        attention_step(L, step)
                        step += 1
                decays(L)
                for j in range(4):
                    split(L, C_OUT_ATT + j + 3)
                ssd(L, 0)
                ssd(L, 1)
                for j in range(3):
                    split(L, C_OUT_SSD + j + 3)
                boundary(L, 8, 3, 4, 1.0, 6)
                split(L, C_OUT_SSD + 3 + 3)
                dve.wait_ge(ple_hi_s, L + 1)
                nc.vector.tensor_tensor(ple_lo_t[:], ple_raw_t[:], ple_hi_t[:].bitcast(F32), ALU.subtract) \
                    .then_inc(ple_lo_s, 1)
                ffn(L, 1)
                boundary(L, 12, 5, 6, 0.5, 8)
                split(L, C_PLE + 2)
                split(L, C_PLE + 3)
                split(L, C_GATE + 3)
                for t in range(TT):
                    dve.wait_ge(gate_ready, L * 2 + t + 1)
                    nc.vector.tensor_tensor(pw[:, t, :], pw[:, t, :], tm[:, t, :], ALU.mult).then_inc(gated, 1)
                for t in range(TT):
                    post(L, 16 + t, 7, t, pw[:, t, :], 1.0)


NORM_TILE = [0, 1, 0, 0, 1, 1, 0, 1, 0, 0, 1, 1, 0, 0, 1, 1, 0, 1]


def buckets():
    rel = CHUNK - 1 - np.arange(191)
    nb = BUCKETS // 2
    ret = (rel > 0).astype(np.int32) * nb
    n = np.abs(rel)
    exact = nb // 2
    large = exact + (np.log(np.maximum(n, 1) / exact) / np.log(WIN / exact) * (nb - exact)).astype(np.int32)
    return ret + np.where(n < exact, n, np.minimum(large, nb - 1))


def constants():
    k = np.arange(P)
    same = (k[:, None] // CHUNK) == (k[None, :] // CHUNK)
    c = np.zeros((P, K_ALL), np.float32)
    c[:, K_ID:K_ID + P] = np.eye(P)
    c[:, K_TRI:K_TRI + P] = same & (k[:, None] <= k[None, :])
    c[:, K_BLK:K_BLK + P] = same
    c[:, K_HALF] = k < CHUNK
    c[:, K_HALF + 1] = k >= CHUNK
    c[buckets(), K_ONEHOT + np.arange(191)] = 1.0
    return c


def lay_out(ffn1_w13, ffn1_w2, ffn2_w13, ffn2_w2, w_in, w_out, ple_w_gate, ple_w_proj):
    out = np.zeros((DEPTH, CHUNKS, P, CW), np.float32)

    def wide(dst, w, cols):
        m = w[:, :, cols].reshape(DEPTH, 2, 4, P, 512).transpose(0, 1, 3, 2, 4)
        out[:, dst:dst + 2] = m.reshape(DEPTH, 2, P, CW)

    def tall(dst, w):
        n = w.shape[1] // (2 * P)
        m = w.reshape(DEPTH, n, 2, P, D).transpose(0, 1, 3, 2, 4)
        out[:, dst:dst + n] = m.reshape(DEPTH, n, P, CW)

    for c0, w in ((C_FFN1, ffn1_w13), (C_FFN2, ffn2_w13)):
        for g in range(GROUPS):
            a = np.arange(g * FW, (g + 1) * FW)
            wide(c0 + 2 * g, w, np.concatenate([a, a + D_FF]))
    tall(C_DOWN1, ffn1_w2)
    tall(C_DOWN2, ffn2_w2)
    z0, xbc0, dt0, q0, k0 = 0, D, D + 1536, D + 1536 + HEADS, 2 * D + 1536 + HEADS
    for k in range(2):
        wide(C_Q + 2 * k, w_in, np.arange(q0 + 512 * k, q0 + 512 * (k + 1)))
        wide(C_Z + 2 * k, w_in, np.arange(z0 + 512 * k, z0 + 512 * (k + 1)))
    wide(C_KV, w_in, np.arange(k0, k0 + 512))
    for k in range(3):
        wide(C_XBC + 2 * k, w_in, np.arange(xbc0 + 512 * k, xbc0 + 512 * (k + 1)))
    dt = w_in[:, :, dt0:dt0 + HEADS].reshape(DEPTH, KT, P, HEADS).transpose(0, 2, 1, 3)
    out[:, C_DT, :, :KT * HEADS] = dt.reshape(DEPTH, P, KT * HEADS)
    tall(C_OUT_ATT, w_out[:, D:])
    tall(C_OUT_SSD, w_out[:, :D])
    tall(C_PLE, ple_w_proj)
    tall(C_GATE, ple_w_gate)
    return out.reshape(DEPTH * CHUNKS * P, CW)


def kernel(x, p, norm_w, ffn1_w13, ffn1_w2, ffn2_w13, ffn2_w2, w_in, conv_w, conv_b, dt_bias, a_log, d_skip,
           ssm_norm_w, attn_sinks, rel_bias_table, w_out, ple_w_gate, ple_w_proj):
    import concourse.bacc as bacc
    from concourse.bass_utils import run_bass_kernel_spmd

    f = lambda a: np.asarray(a)
    rows = np.concatenate([f(norm_w), f(ssm_norm_w)[:, None]], axis=1).reshape(DEPTH * (NORMS + 1), D)
    params = np.zeros((DEPTH, P, A_ALL), np.float32)
    params[:, :, A_CW:A_CW + 48] = f(conv_w).reshape(DEPTH, CONVW, CT, P).transpose(0, 3, 2, 1).reshape(DEPTH, P, 48)
    params[:, :, A_CB:A_CB + CT] = f(conv_b).reshape(DEPTH, CT, P).transpose(0, 2, 1)
    sinks = f(attn_sinks).reshape(DEPTH, KV, 2, 2).transpose(0, 1, 3, 2).reshape(DEPTH, HEADS)
    for at, a in ((A_DTB, dt_bias), (A_ALOG, a_log), (A_DSKIP, d_skip), (A_SINK, sinks)):
        params[:, :, at:at + HEADS] = f(a)[:, None, :]
    arrays = {
        "x": f(x).reshape(SEQ, D),
        "chunks": lay_out(*(f(a) for a in (ffn1_w13, ffn1_w2, ffn2_w13, ffn2_w2, w_in, w_out,
                                           ple_w_gate, ple_w_proj))),
        "ple": np.ascontiguousarray(f(p).reshape(DEPTH, SEQ, PLE).transpose(0, 2, 1)).reshape(DEPTH * PLE, SEQ),
        "rows": np.ascontiguousarray(rows),
        "params": params.reshape(DEPTH * P, A_ALL),
        "table": f(rel_bias_table),
        "consts": constants(),
    }
    nc = bacc.Bacc("TRN2", target_bir_lowering=False, num_devices=1, dynamic_dma_scratch_size=4096)
    args = [nc.dram_tensor(f"in_{n}", a.shape, mybir.dt.from_np(a.dtype), kind="ExternalInput").ap()
            for n, a in arrays.items()]
    args.append(nc.dram_tensor("out_x", (SEQ, D), F32, kind="ExternalOutput").ap())
    trunk(nc, *args)
    r = run_bass_kernel_spmd(nc, [{f"in_{n}": a for n, a in arrays.items()}], core_ids=[0])
    return r.results[0]["out_x"].reshape(1, SEQ, D)
```

```python
import math
from contextlib import ExitStack

import numpy as np
import concourse.bass as bass
from concourse import mybir

F32 = mybir.dt.float32
F32R = mybir.dt.float32r
ALU = mybir.AluOpType
ACT = mybir.ActivationFunctionType
AX = mybir.AxisListType.X

P = 128
D = 1024
SEQ = 256
DEPTH = 2
TT = SEQ // P
KT = D // P
D_FF = 2816
HT = D_FF // P
FW = 256
GROUPS = D_FF // FW
PLE = 256
EPS = 1e-6
NORMS = 8
CHUNK = 64
HEADS = 16
HD = 64
STATE = 128
CONVW = 4
CT = 12
KV = 4
BUCKETS = 32
WIN = 128
SCALE = 1.0 / math.sqrt(HD)
MASKED = -1.0e30

CW = 2048
RING = 4
C_FFN1 = 0
C_DOWN1 = C_FFN1 + 2 * GROUPS
C_KV = C_DOWN1 + HT // 2
C_DT = C_KV + 2
C_Q = C_DT + 1
C_XBC = C_Q + 4
C_Z = C_XBC + 6
C_OUT_ATT = C_Z + 4
C_OUT_SSD = C_OUT_ATT + 4
C_FFN2 = C_OUT_SSD + 4
C_DOWN2 = C_FFN2 + 2 * GROUPS
C_PLE = C_DOWN2 + HT // 2
C_GATE = C_PLE + 1
CHUNKS = C_GATE + 4
AHEAD = 3
EARLY = 2
assert CHUNKS % RING == 0
LOADS = CHUNKS // RING

K_ID, K_TRI, K_BLK, K_HALF, K_ONEHOT = 0, P, 2 * P, 3 * P, 3 * P + 2
K_ALL = K_ONEHOT + WIN + CHUNK - 1
REL = WIN + CHUNK


A_CW, A_CB, A_DTB, A_ALOG, A_DSKIP, A_SINK = 0, 48, 60, 76, 92, 108
A_ALL = 124

N_T0 = 2 * (GROUPS + 1) + 2 + 1 + 1 + 1
N_NORM = 18
N_UT = 2 * 10
N_YH = 2 * 3
N_X = 2 * 4
N_WIN = 8
W_KV, W_Q, W_XBC, W_Z = 0, 1, 3, 6
N_H = 2 * 2 * GROUPS
N_HT = 2 * GROUPS
N_ITEM = TT * KV

T0_FFN = (0, GROUPS + 4)
T0_DOWN = (GROUPS, 2 * GROUPS + 4)
T0_Z = GROUPS + 1
T0_OUT = GROUPS + 3
T0_PLE = 2 * GROUPS + 5
T0_GATE = 2 * GROUPS + 6
assert T0_GATE + 1 == N_T0

SS_PARTS = [1, 1] + [2, 1, 2, 1] + [2, 2] + 2 * [2, 1, 2, 1] + [2, 2]
SS_DONE = [sum(SS_PARTS[:n + 1]) for n in range(N_NORM)]
N_SS = SS_DONE[-1]
RMS_D = math.sqrt(D)

FFN_NORM = ((0, 1), (9, 11))
Y_NTH = {2: 0, 4: 1, 8: 2, 10: 3, 12: 4, 14: 5}

ROW_SSM = NORMS
ROW_SLOT = {1: 1, 2: 0, ROW_SSM: 1, 3: 0, 4: 1, 5: 0, 6: 1, 7: 0}
ROW_LOADS = {0: 4, 1: 4}
ROW_NTH = {2: 1, 3: 2, 5: 3, 7: 4, 1: 1, ROW_SSM: 2, 4: 3, 6: 4}


def trunk(nc, x_in, chunks_in, ple_in, rows_in, params_in, table_in, consts_in, rel_bias, out):
    ctx = ExitStack()
    with ctx:
        at = {"o": -(-nc.sbuf_base // 64) * 64}

        def place(name, cols, dt=F32, offset=None):
            o = at["o"] if offset is None else offset
            t = nc.alloc_sbuf_tensor_at(name, [P, cols], dt, offset=o)
            if offset is None:
                at["o"] = o + -(-cols * 4 // 32) * 32
            return t

        def sem(name):
            return ctx.enter_context(nc.semaphore(name))

        stage = [place(f"stage{s}", CW) for s in range(RING)]
        w_hi = [place(f"w_hi{s}", CW, F32R) for s in range(RING)]
        w_lo = [place(f"w_lo{s}", CW, F32R) for s in range(RING)]
        x_sb = place("x_sb", TT * D)[:].rearrange("p (t n) -> p t n", t=TT)
        tm = place("tm", TT * D)[:].rearrange("p (t n) -> p t n", t=TT)
        uT_hi_t = place("uT_hi", KT * SEQ, F32R)
        uT_lo_t = place("uT_lo", KT * SEQ, F32R)
        rows = [place(f"row{s}", D) for s in range(2)]
        bias = place("bias", HEADS * WIN)[:].rearrange("p (h j) -> p h j", h=HEADS)
        consts = place("consts", K_ALL)
        consts16 = place("consts16", P)[:].bitcast(mybir.dt.bfloat16)
        params = place("params", A_ALL)
        table = place("table", HEADS)
        ss = place("ss", 2 * N_NORM)
        var = place("var", 2)
        rstd = place("rstd", N_NORM)
        half_neg = place("half_neg", 1)
        d_eps = place("d_eps", 1)
        soft = place("soft", 16)
        dts = place("dts", 10 * 32)
        att_s = place("att_s", 2 * 5 * KV)
        region = at["o"]
        hT_hi_t = place("hT_hi", HT * SEQ, F32R, region)
        hT_lo_t = place("hT_lo", HT * SEQ, F32R, region + HT * SEQ * 4)
        sg_t = place("sg", 2 * TT * FW, F32, region + 2 * HT * SEQ * 4)
        hs_t = place("hs", 2 * TT * FW, F32, region + 2 * HT * SEQ * 4 + 2 * TT * FW * 4)
        pw_t = place("pw", TT * D, F32, region)
        ple_raw_t = place("ple_raw", 2 * SEQ, F32, region + 2 * HT * SEQ * 4 + 4 * TT * FW * 4)
        ple_hi_t = place("ple_hi", 2 * SEQ, F32R, region + 2 * HT * SEQ * 4 + 4 * TT * FW * 4 + 2 * SEQ * 4)
        ple_lo_t = place("ple_lo", 2 * SEQ, F32R, region + 2 * HT * SEQ * 4 + 4 * TT * FW * 4 + 4 * SEQ * 4)
        row0 = place("row0", D, F32, region + 2 * HT * SEQ * 4 + 4 * TT * FW * 4)
        squares_t = place("squares", 3 * D, F32, region + 2 * HT * SEQ * 4 + 4 * TT * FW * 4 + 6 * SEQ * 4)
        mix_cols = CT * SEQ + 2048 + 1024 + 2048 + 2048 + 1024 + 2048
        mix = place("mix", mix_cols, F32, region)
        attT_hi_t = place("attT_hi", KT * SEQ, F32R, region + mix_cols * 4)
        attT_lo_t = place("attT_lo", KT * SEQ, F32R, region + mix_cols * 4 + KT * SEQ * 4)
        assert region + mix_cols * 4 + 2 * KT * SEQ * 4 <= nc.sbuf_usable_end

        def tiles(t, k):
            return t[:].rearrange("p (k n) -> p k n", k=k)

        uT_hi, uT_lo = tiles(uT_hi_t, KT), tiles(uT_lo_t, KT)
        hT_hi, hT_lo = tiles(hT_hi_t, HT), tiles(hT_lo_t, HT)
        attT_hi, attT_lo = tiles(attT_hi_t, KT), tiles(attT_lo_t, KT)
        ple_hi, ple_lo = tiles(ple_hi_t, 2), tiles(ple_lo_t, 2)
        pw = tiles(pw_t, TT)
        sg = sg_t[:].rearrange("p (b t n) -> p b t n", b=2, t=TT)
        hs = hs_t[:].rearrange("p (b t n) -> p b t n", b=2, t=TT)
        squares = squares_t[:].bitcast(mybir.dt.bfloat16).rearrange("p (b n) -> p b n", b=6)

        o = 0
        raw = mix[:, o:o + CT * SEQ].rearrange("p (c n) -> p c n", c=CT)
        o += CT * SEQ
        qT = mix[:, o:o + 2048].rearrange("p (k n) -> p k n", k=8)
        xs = mix[:, o:o + 2048].rearrange("p (t n) -> p t n", t=TT)
        o += 2048
        kdup = mix[:, o:o + 1024].rearrange("p (k n) -> p k n", k=KV)
        xd = mix[:, o:o + 1024]
        o += 1024
        vwin = mix[:, o:o + 2048].rearrange("p (c k u d) -> p c k u d", c=4, k=KV, u=2)
        btok = mix[:, o:o + 256].rearrange("p (g n) -> p g n", g=2)
        cbm = mix[:, o + 256:o + 512].rearrange("p (g n) -> p g n", g=2)
        o += 2048
        zs = mix[:, o:o + 2048].rearrange("p (t n) -> p t n", t=TT)
        o += 2048
        acc = mix[:, o:o + 1024]
        o += 1024
        lg = mix[:, o:o + 1024].rearrange("p (b h j) -> p b h j", b=2, h=4)
        pT = mix[:, o + 1024:o + 2048].rearrange("p (b n) -> p b n", b=2)
        hst = mix[:, o:o + 1024]
        seg = mix[:, o + 1024:o + 2048].rearrange("p (b h l) -> p b h l", b=2, h=4)

        ident = consts[:, K_ID:K_ID + P]
        tri = consts[:, K_TRI:K_TRI + P]
        blk = consts[:, K_BLK:K_BLK + P]
        ident16 = consts16[:, 0:P]
        mask16 = consts16[:, P:2 * P]

        def small(i):
            return dts[:, 32 * i:32 * i + 32]

        S_DTR, S_V, S_W, S_DT, S_ADT, S_NCS, S_ECS, S_EDEC, S_DEC0, S_DEC1 = range(10)

        psA = ctx.enter_context(nc.psum_tensor("psA", [P, 2, 512], F32))
        psB = ctx.enter_context(nc.psum_tensor("psB", [P, 2, 512], F32))
        psC = ctx.enter_context(nc.psum_tensor("psC", [P, 2, 512], F32))
        psD = ctx.enter_context(nc.psum_tensor("psD", [P, 2, 512], F32))
        gemm = [psA, psB]
        turn = [psC, psD]

        ident_in = sem("ident_loaded")
        setup_in = sem("setup_in")
        x_half = sem("x_half")
        x_in_s = [sem(f"x_loaded{t}") for t in range(TT)]
        masks_ready = sem("masks_ready")
        params_in_s = sem("params_loaded")
        ple_loaded = sem("ple_loaded")
        row0_first = sem("row0_first")
        row0_loaded = sem("row0_loaded")
        row_loaded = [sem(f"row_loaded{s}") for s in range(2)]
        out_stored = sem("out_stored")
        stage_full = [sem(f"stage_full{s}") for s in range(RING)]
        hi_ready = sem("hi_ready")
        lo_ready = sem("lo_ready")
        w_used = sem("w_used")
        gemm_t0 = sem("gemm_t0")
        bias_ps = sem("bias_ps")
        bias_sb = sem("bias_sb")
        bias_stored = sem("bias_stored")
        bias_loaded = sem("bias_loaded")
        silu_ready = sem("silu_ready")
        h_ready = sem("h_ready")
        hT_ps = sem("hT_ps")
        hT_hi_s = sem("hT_hi_ready")
        hT_lo_s = sem("hT_lo_ready")
        ss_ready = sem("ss_ready")
        rstd_ready = sem("rstd_ready")
        y_half = sem("y_half")
        u_ready = sem("u_ready")
        x_ready = sem("x_ready")
        uT_ps = sem("uT_ps")
        uT_hi_s = sem("uT_hi_ready")
        uT_lo_s = sem("uT_lo_ready")
        ple_hi_s = sem("ple_hi_ready")
        ple_lo_s = sem("ple_lo_ready")
        pw_ready = sem("pw_ready")
        gate_ready = sem("gate_ready")
        gated = sem("gated")
        win_evac = sem("win_evac")
        conv_acc = sem("conv_acc")
        conv_ready = sem("conv_ready")
        score_ps = sem("score_ps")
        logit_ready = sem("logit_ready")
        exp_ready = sem("exp_ready")
        prob_ready = sem("prob_ready")
        pT_ps = sem("pT_ps")
        pT_ready = sem("pT_ready")
        pv_ps = sem("pv_ps")
        att_hi_s = sem("att_hi_ready")
        att_lo_s = sem("att_lo_ready")
        a_ready = sem("a_ready")
        dt_rows = sem("dt_rows")
        dt_ps = sem("dt_ps")
        dt_ready = sem("dt_ready")
        dtv_ready = sem("dtv_ready")
        dexp_ready = sem("dexp_ready")
        ratio_ready = sem("ratio_ready")
        adt_ready = sem("adt_ready")
        cs_ps = sem("cs_ps")
        cs_ready = sem("cs_ready")
        dec_ready = sem("dec_ready")
        xT_ps = sem("xT_ps")
        xb_ready = sem("xb_ready")
        cb_ps = sem("cb_ps")
        off_ps = sem("off_ps")
        off_out = sem("off_out")
        st_ps = sem("st_ps")
        st_ready = sem("st_ready")
        seg_ps = sem("seg_ps")
        dec_mat = sem("dec_mat")
        m_ready = sem("m_ready")
        diag_ps = sem("diag_ps")
        yg_ready = sem("yg_ready")

        block = ctx.enter_context(nc.Block())

        def conv_sums(b):
            return (zs[:, 0, :], acc, zs[:, 0, :])[b].rearrange("p (c n) -> p c n", c=4)

        def item(n):
            return (n // 2) % TT, n % 2 + 2 * (n // 4)

        def att_views(attT, t, kv, par):
            r = slice(HD * par, HD * par + HD)
            dst = attT[r, 2 * kv:2 * kv + 2, t * P:t * P + P].rearrange("p k (f q) -> p k f q", f=2)
            src = psD[r, 1, :].rearrange("p (f u k q) -> p u k f q", f=2, k=2, u=2)[:, par]
            return dst, src

        def chunk_cols(c):
            return slice(0, KT * HEADS if c == C_DT else CW)

        def stage_value(L, c, i):
            return L * (16 * LOADS) + i * 16 + 16 * (c // RING + 1)

        def chunk_value(L, c, i):
            return L * CHUNKS + i * RING + c + 1

        @block.sync
        def _(sp):
            x_view = x_in.rearrange("(t p) n -> p t n", p=P)
            sp.dma_start(x_sb[:, 0, :], x_view[:, 0, :]).then_inc(x_in_s[0], 16)
            sp.dma_start(ident, consts_in[:, K_ID:K_ID + P]).then_inc(ident_in, 16)

            def load_chunks(i):
                for s in range(RING):
                    sp.wait_ge(lo_ready, i * RING + s + 1)
                    sp.dma_start(stage[s][:], chunks_in[bass.ds((i * RING + s) * P, P), :]).then_inc(stage_full[s], 16)
                    if isinstance(i, int) and s == 0:
                        sp.dma_start(row0[:], rows_in[0:1, :].broadcast_to([P, D])).then_inc(row0_first, 16)
                        sp.dma_start(consts[:, K_TRI:], consts_in[:, K_TRI:]).then_inc(setup_in, 16)
                        sp.dma_start(table[0:BUCKETS, :], table_in).then_inc(setup_in, 16)
                    if isinstance(i, int) and s == 1:
                        sp.dma_start(x_sb[:, 1, :], x_view[:, 1, :]).then_inc(x_in_s[1], 16)

            load_chunks(0)
            with sp.Fori(1, 4) as i:
                load_chunks(i)
            sp.wait_ge(bias_sb, 1)
            copies = rel_bias.rearrange("(q n) -> q n", q=CHUNK)[:, 0:HEADS * REL]
            sp.dma_start(copies.rearrange("q (h w) -> h q w", w=REL)[:, :, 0:REL - 1],
                         dts[0:HEADS, 0:REL - 1].rearrange("h (q w) -> h q w", q=1)
                         .broadcast_to([HEADS, CHUNK, REL - 1])).then_inc(bias_stored, 16)
            sp.wait_ge(bias_stored, 16)
            shifted = rel_bias[CHUNK - 1:CHUNK - 1 + CHUNK * HEADS * REL].rearrange("(q h w) -> q h w", q=CHUNK, w=REL)
            for u in range(2):
                sp.dma_start(bias[CHUNK * u:CHUNK * u + CHUNK], shifted[:, :, 0:WIN]).then_inc(bias_loaded, 16)
            with sp.Fori(4, DEPTH * LOADS) as i:
                load_chunks(i)
            for s in range(EARLY):
                sp.wait_ge(lo_ready, DEPTH * CHUNKS + s + 1)
                sp.nop().then_inc(stage_full[s], 16)
            out_view = out.rearrange("(t p) n -> p t n", p=P)
            sp.wait_ge(x_ready, N_X * DEPTH + 1)
            sp.dma_start(out_view[:, 0, :], x_sb[:, 0, :]).then_inc(out_stored, 16)
            for half in range(2):
                w = slice(512 * half, 512 * half + 512)
                if half == 0:
                    sp.wait_ge(x_half, DEPTH)
                else:
                    sp.wait_ge(x_ready, N_X * DEPTH + 2)
                sp.dma_start(out_view[:, 1, w], x_sb[:, 1, w]).then_inc(out_stored, 16)
            sp.wait_ge(out_stored, 48)

        @block.gpsimd
        def _(pool):
            nc.gpsimd.memset(half_neg[:], -0.5)
            nc.gpsimd.memset(d_eps[:], D * EPS)
            pool.drain()

            def load_row(L, r):
                s = ROW_SLOT[r]
                src = rows_in[bass.ds(L * (NORMS + 1) + r, 1), :].broadcast_to([P, D])
                pool.dma_start(rows[s][:], src).then_inc(row_loaded[s], 16)

            def inverse_roots(L, first, n):
                for k in range(first, first + n):
                    v = var[:, k % 2:k % 2 + 1]
                    for part in range(SS_PARTS[k]):
                        pool.wait_ge(ss_ready, L * N_SS + SS_DONE[k] - SS_PARTS[k] + part + 1)
                        nc.gpsimd.tensor_tensor(v, v if part else d_eps[:], ss[:, 2 * k + part:2 * k + part + 1],
                                                ALU.add)
                        pool.drain()
                    nc.gpsimd.tensor_tensor(rstd[:, k:k + 1], v, half_neg[:], ALU.pow).then_inc(rstd_ready, 1)

            def inputs_done(L, n):
                pool.wait_ge(u_ready, L * N_UT + 2 * n)

            def outputs_done(L, n):
                pool.wait_ge(x_ready, L * N_X + TT + n)

            def fence():
                pool.drain()

            def conv(L, b):
                pool.wait_ge(win_evac, L * N_WIN + W_XBC + b + 1)
                a = conv_sums(b)
                product = zs[:, 1, :].rearrange("p (c n) -> p c n", c=4)
                x4 = raw[:, 4 * b:4 * b + 4, :]
                weights = params[:, A_CW + 16 * b:A_CW + 16 * b + 16].rearrange("p (c k) -> p k c", k=CONVW)
                offsets = params[:, A_CB + 4 * b:A_CB + 4 * b + 4]

                def over_tokens(ap, n):
                    return ap.rearrange("p (c u) -> p c u", u=1).broadcast_to([P, 4, n])

                nc.gpsimd.tensor_tensor(a, x4, over_tokens(weights[:, CONVW - 1], SEQ), ALU.mult)
                fence()
                nc.gpsimd.tensor_tensor(a, a, over_tokens(offsets, SEQ), ALU.add)
                for tap in (2, 1, 0):
                    d = CONVW - 1 - tap
                    nc.gpsimd.tensor_tensor(product[:, :, d:], x4[:, :, :SEQ - d],
                                            over_tokens(weights[:, tap], SEQ - d), ALU.mult)
                    fence()
                    last = nc.gpsimd.tensor_tensor(a[:, :, d:], a[:, :, d:], product[:, :, d:], ALU.add)
                    if tap:
                        fence()
                last.then_inc(conv_acc, 1)

            def dt_back(L):
                pool.wait_ge(ratio_ready, L + 1)
                r, s2, p_ = small(S_DTR), small(S_ECS), small(S_EDEC)
                nc.gpsimd.tensor_tensor(s2, r, r, ALU.mult)
                fence()
                nc.gpsimd.tensor_scalar(p_, s2, 2.0 / 15, 2.0 / 13, ALU.mult, ALU.add)
                for n in (11, 9, 7, 5, 3, 1):
                    fence()
                    nc.gpsimd.tensor_tensor(p_, p_, s2, ALU.mult)
                    fence()
                    nc.gpsimd.tensor_scalar(p_, p_, 2.0 / n, None, ALU.add)
                fence()
                nc.gpsimd.tensor_tensor(p_, p_, r, ALU.mult)
                fence()
                nc.gpsimd.tensor_tensor(small(S_DT), small(S_DT), p_, ALU.add)
                fence()
                pool.wait_ge(a_ready, L + 1)
                for t in range(TT):
                    sl = slice(32 * S_DT + 16 * t, 32 * S_DT + 16 * t + 16)
                    so = slice(32 * S_ADT + 16 * t, 32 * S_ADT + 16 * t + 16)
                    nc.gpsimd.tensor_tensor(dts[:, so], dts[:, sl], soft[:], ALU.mult)
                fence()
                nc.gpsimd.tensor_scalar(small(S_ADT), small(S_ADT), -1.0, None, ALU.mult).then_inc(adt_ready, 1)

            pool.wait_ge(row0_first, 16)
            with pool.Fori(0, DEPTH) as L:
                load_row(L, 1)
                pool.dma_start(params[:], params_in[bass.ds(L * P, P), :]).then_inc(params_in_s, 16)
                load_row(L, 2)
                inverse_roots(L, 0, 2)
                inverse_roots(L, 2, 4)
                outputs_done(L, 2)
                load_row(L, ROW_SSM)
                inputs_done(L, 4)
                load_row(L, 3)
                dt_back(L)
                conv(L, 0)
                conv(L, 1)
                inverse_roots(L, 6, 2)
                inputs_done(L, 6)
                load_row(L, 4)
                inverse_roots(L, 8, 4)
                outputs_done(L, 4)
                load_row(L, 5)
                inputs_done(L, 8)
                load_row(L, 6)
                pool.wait_ge(w_used, L * CHUNKS + C_OUT_SSD + 4 + RING)
                pool.dma_start(ple_raw_t[:].rearrange("p (k n) -> p k n", k=2),
                               ple_in[bass.ds(L * PLE, PLE), :].rearrange("(k p) n -> p k n", p=P)) \
                    .then_inc(ple_loaded, 16)
                inverse_roots(L, 12, 4)
                outputs_done(L, 6)
                load_row(L, 7)
                pool.wait_ge(w_used, L * CHUNKS + C_PLE + 1 + RING)
                pool.dma_start(row0[:], rows_in[bass.ds((L + 1) * (NORMS + 1), 1), :].broadcast_to([P, D])) \
                    .then_inc(row0_loaded, 16)
                inverse_roots(L, 16, 2)
                inputs_done(L, 10)
                outputs_done(L, 8)

        @block.tensor
        def _(pe):
            nc.tensor.nop().then_inc(w_used, RING)

            def chunk_ready(L, c, i=0):
                pe.wait_ge(lo_ready, chunk_value(L, c, i) + RING)

            def three(out_ap, hi, lo, whi, wlo, start, stop, moving_weights=True):
                if moving_weights:
                    nc.tensor.matmul(out_ap, hi, whi, start=start, stop=False, skip_group_check=True)
                    nc.tensor.matmul(out_ap, lo, whi, start=False, stop=False, skip_group_check=True)
                    return nc.tensor.matmul(out_ap, hi, wlo, start=False, stop=stop, skip_group_check=True)
                nc.tensor.matmul(out_ap, whi, hi, start=start, stop=False, skip_group_check=True)
                nc.tensor.matmul(out_ap, whi, lo, start=False, stop=False, skip_group_check=True)
                return nc.tensor.matmul(out_ap, wlo, hi, start=False, stop=stop, skip_group_check=True)

            def wide_half(ps, t, slot, half):
                for k in range(4):
                    kt = 4 * half + k
                    w = slice(512 * k, 512 * k + 512)
                    mm = three(ps, uT_hi[:, kt, t * P:t * P + P], uT_lo[:, kt, t * P:t * P + P],
                               w_hi[slot][:, w], w_lo[slot][:, w], kt == 0, kt == KT - 1)
                return mm

            def transposes(dst, src, n):
                for k in range(n):
                    mm = nc.tensor.transpose(dst[:, k * P:k * P + P], src[:, k * P:k * P + P], ident)
                return mm

            def u_transposes(L, n):
                t = n % 2
                for half in range(2):
                    pe.wait_ge(u_ready, L * N_UT + 2 * n + half + 1)
                    transposes(turn[t][:, half, :], tm[:, t, 512 * half:512 * half + 512], 4).then_inc(uT_ps, 1)

            def wait_uT(L, n, half=1):
                pe.wait_ge(uT_lo_s, L * N_UT + 2 * n + half + 1)

            def ffn_group(L, f, c, i):
                ps = gemm[((c - (C_FFN1, C_FFN2)[f]) // 2) % 2]
                for half in range(2):
                    s = (c + half) % RING
                    chunk_ready(L, c + half, i)
                    mm = wide_half(ps[:, 0, :], 0, s, half)
                    if half:
                        mm.then_inc(gemm_t0, 1)
                    wide_half(ps[:, 1, :], 1, s, half).then_inc(w_used, 1)

            def h_transposes(L, par, done):
                pe.wait_ge(h_ready, L * N_H + done)
                ps = turn[par][:, 0, :].rearrange("p (k t n) -> p k t n", k=2, t=TT)
                for t in range(TT):
                    for k in range(2):
                        mm = nc.tensor.transpose(ps[:, k, t, :], hs[:, par, t, k * P:k * P + P], ident)
                mm.then_inc(hT_ps, 1)

            def k_chunk(L, c, t, hi, lo, kt0, last_kt, first, between=None):
                s = c % RING
                for k in range(2):
                    if k and between:
                        between()
                    for half in range(2):
                        w = slice(k * D + half * 512, k * D + half * 512 + 512)
                        mm = three(first[t][:, half, :], hi[:, kt0 + k, t * P:t * P + P],
                                   lo[:, kt0 + k, t * P:t * P + P], w_hi[s][:, w], w_lo[s][:, w],
                                   (c, k) == first["start"], kt0 + k == last_kt)
                return mm

            def ffn(L, f):
                c0 = (C_FFN1, C_FFN2)[f]
                cd = (C_DOWN1, C_DOWN2)[f]
                hb = f * 2 * GROUPS
                ps = gemm[0]
                n = (0, 6)[f]
                for half in range(2):
                    wait_uT(L, n, half)
                    chunk_ready(L, c0 + half)
                    mm = wide_half(ps[:, 0, :], 0, (c0 + half) % RING, half)
                mm.then_inc(gemm_t0, 1)
                u_transposes(L, n + 1)
                for half in range(2):
                    wait_uT(L, n + 1, half)
                    wide_half(ps[:, 1, :], 1, (c0 + half) % RING, half).then_inc(w_used, 1)
                with pe.Fori(0, (GROUPS - 1) // 2) as i:
                    for par in (1, 0):
                        g0 = 2 - par
                        ffn_group(L, f, c0 + 2 * g0, i)
                        h_transposes(L, 1 - par, hb + i * 4 + 2 * g0)
                out2 = {0: gemm[0], 1: gemm[1], "start": (cd, 0)}
                chunk_ready(L, cd)
                pe.wait_ge(hT_lo_s, L * N_HT + f * GROUPS + 1)
                k_chunk(L, cd, 1, hT_hi, hT_lo, 0, HT - 1, out2)
                h_transposes(L, 0, hb + 2 * GROUPS)
                k_chunk(L, cd, 0, hT_hi, hT_lo, 0, HT - 1, out2).then_inc(w_used, 1)
                pe.wait_ge(hT_lo_s, L * N_HT + f * GROUPS + GROUPS - 1)
                for j in range(1, GROUPS - 4):
                    chunk_ready(L, cd + j)
                    k_chunk(L, cd + j, 0, hT_hi, hT_lo, 2 * j, HT - 1, out2)
                    k_chunk(L, cd + j, 1, hT_hi, hT_lo, 2 * j, HT - 1, out2).then_inc(w_used, 1)
                pe.wait_ge(hT_lo_s, L * N_HT + f * GROUPS + GROUPS)
                output_tail(L, cd + GROUPS - 4, hT_hi, hT_lo, HT - 8, out2,
                            under=lambda: u_transposes(L, (2, 8)[f]))

            def win_free(L, k):
                if k >= 2:
                    pe.wait_ge(win_evac, L * N_WIN + k - 1)

            def turned_half(ps, m0, ms, slot, half):
                for m in ms:
                    for k in range(4):
                        w = slice(512 * k + P * m, 512 * k + P * m + P)
                        mm = three(ps[:, (m - m0) // 2, ((m - m0) % 2) * SEQ:((m - m0) % 2 + 1) * SEQ],
                                   uT_hi[:, 4 * half + k, :], uT_lo[:, 4 * half + k, :],
                                   w_hi[slot][:, w], w_lo[slot][:, w],
                                   half == 0 and k == 0 and (m - m0) % 2 == 0,
                                   half == 1 and k == 3, moving_weights=False)
                return mm

            def turned_chunk(L, k, c, half):
                if half == 0:
                    win_free(L, k)
                chunk_ready(L, c + half)
                turned_half(gemm[k % 2], 0, range(3), (c + half) % RING, half)
                if half == 0 and k == W_Q + 1:
                    pe.wait_ge(win_evac, L * N_WIN + W_Q + 1)
                    pe.wait_ge(dt_ready, L + 1)
                if half == 1 and k == W_Q:
                    pe.wait_ge(dt_rows, L + 1)
                if half == 0 and k == W_XBC + 1:
                    pe.wait_ge(win_evac, L * N_WIN + W_Q + 2)
                turned_half(gemm[k % 2], 0, (3,), (c + half) % RING, half).then_inc(w_used, 1)

            def v_part(t, half):
                s = (C_KV + half) % RING
                for k in range(4):
                    kt = 4 * half + k
                    w = slice(512 * k + 256, 512 * k + 512)
                    mm = three(gemm[0][:, 1, 256 * t:256 * t + 256], uT_hi[:, kt, t * P:t * P + P],
                               uT_lo[:, kt, t * P:t * P + P], w_hi[s][:, w], w_lo[s][:, w],
                               kt == 0 and t == 0, kt == KT - 1)
                return mm

            def k_v(L):
                for half in range(2):
                    wait_uT(L, 2, half)
                    chunk_ready(L, C_KV + half)
                    v_part(0, half)
                u_transposes(L, 3)
                for half in range(2):
                    wait_uT(L, 3, half)
                    turned_half(gemm[0], 0, range(2), (C_KV + half) % RING, half)
                    v_part(1, half).then_inc(w_used, 1)

            def dt_product(L):
                chunk_ready(L, C_DT)
                s = C_DT % RING
                for kt in range(KT):
                    w = slice(HEADS * kt, HEADS * kt + HEADS)
                    mm = three(psD[0:HEADS, 0, 0:SEQ], uT_hi[:, kt, :], uT_lo[:, kt, :], w_hi[s][:, w],
                               w_lo[s][:, w], kt == 0, kt == KT - 1, moving_weights=False)
                mm.then_inc(w_used, 1)

            def dt_turn(L):
                for t in range(TT):
                    mm = nc.tensor.transpose(psC[:, 0, HEADS * t:HEADS * t + HEADS],
                                             raw[0:HEADS, 0, t * P:t * P + P], ident[0:HEADS, 0:HEADS])
                mm.then_inc(dt_ps, 1)

            def z_part(L, k, half, t):
                g, c = W_Z + k, C_Z + 2 * k + half
                if t == 0:
                    if half == 0:
                        win_free(L, g)
                    chunk_ready(L, c)
                mm = wide_half(gemm[g % 2][:, t, :], t, c % RING, half)
                if t == 1:
                    mm.then_inc(w_used, 1)
                elif half:
                    mm.then_inc(gemm_t0, 1)

            def scores(L, n):
                t, kv = item(n)
                for hf in range(2):
                    c = 2 * t + hf
                    lo_tok = max(c - 1, 0) * CHUNK
                    width = (c + 1) * CHUNK - lo_tok
                    for hh in range(4):
                        h = 4 * kv + hh
                        po = HD * (h % 2)
                        mm = nc.tensor.matmul(
                            psC[CHUNK * hf:CHUNK * hf + CHUNK, hh % 2,
                                WIN * (hh // 2) + WIN - width:WIN * (hh // 2) + WIN],
                            qT[po:po + HD, h // 2, c * CHUNK:c * CHUNK + CHUNK],
                            kdup[po:po + HD, kv, lo_tok:lo_tok + width], start=True, stop=True)
                mm.then_inc(score_ps, 1)

            def prob_transposes(L, n):
                pe.wait_ge(prob_ready, L * N_ITEM + n + 1)
                if n >= 1:
                    pe.wait_ge(pT_ready, L * N_ITEM + n)
                transposes(psD[:, 0, :], lg[:, n % 2].rearrange("p h j -> p (h j)"), 4).then_inc(pT_ps, 1)

            def values(L, n):
                t, kv = item(n)
                pe.wait_ge(pT_ready, L * N_ITEM + n + 1)
                if n >= 1:
                    pe.wait_ge(att_lo_s, L * N_ITEM + n)
                probs = pT[:, n % 2].rearrange("p (h q) -> p h q", h=4)
                for hf in range(2):
                    v = vwin[:, 2 * t + hf, kv].rearrange("p u d -> p (u d)")
                    mm = nc.tensor.matmul(psD[:, 1, 256 * hf:256 * hf + 256], v,
                                          probs[:, :, hf * CHUNK:hf * CHUNK + CHUNK], start=True, stop=True)
                mm.then_inc(pv_ps, 1)

            def attention_step(L, n):
                if 1 <= n <= N_ITEM:
                    prob_transposes(L, n - 1)
                if 0 <= n < N_ITEM:
                    scores(L, n)
                if 2 <= n <= N_ITEM + 1:
                    values(L, n - 2)

            def decay_sums(L):
                pe.wait_ge(adt_ready, L + 1)
                adt = small(S_ADT)
                nc.tensor.matmul(psC[:, 0, 0:32], tri, adt, start=True, stop=True)
                nc.tensor.matmul(psC[:, 0, 32:64], blk, adt, start=True, stop=True)
                for hf in range(2):
                    ind = consts[:, K_HALF + hf:K_HALF + hf + 1].broadcast_to([P, P])
                    mm = nc.tensor.matmul(psC[:, 0, 64 + 32 * hf:96 + 32 * hf], ind, adt, start=True, stop=True)
                mm.then_inc(cs_ps, 1)

            def ssd_turn(L, t):
                if t == 0:
                    pe.wait_ge(conv_ready, L * 3 + 3)
                    pe.wait_ge(cs_ready, L + 1)
                    pe.wait_ge(att_lo_s, L * N_ITEM + N_ITEM)
                else:
                    pe.wait_ge(yg_ready, L * 4 + 2)
                for k in range(8):
                    nc.tensor.transpose(psC[:, k // 4, (k % 4) * P:(k % 4 + 1) * P],
                                        raw[:, k, t * P:t * P + P], ident)
                for g in range(2):
                    mm = nc.tensor.transpose(psD[:, 0, g * P:g * P + P], raw[:, 8 + g, t * P:t * P + P], ident)
                mm.then_inc(xT_ps, 1)
                for g in range(2):
                    mm = nc.tensor.matmul(psD[:, 1, g * P:g * P + P], raw[:, 8 + g, t * P:t * P + P],
                                          raw[:, 10 + g, t * P:t * P + P], start=True, stop=True)
                mm.then_inc(cb_ps, 1)

            def ssd_off(L, t, hf):
                c = 2 * t + hf
                pe.wait_ge(st_ready, L * 3 + c)
                if hf == 0 or c == 1:
                    pe.wait_ge(xb_ready, L * 4 + 2 * t + 2)
                for g in range(2):
                    mm = nc.tensor.matmul(psD[CHUNK * hf:CHUNK * hf + CHUNK, g, :],
                                          raw[:, 10 + g, c * CHUNK:c * CHUNK + CHUNK],
                                          hst[:, 512 * g:512 * g + 512], start=True, stop=True)
                mm.then_inc(off_ps, 1)

            def ssd_state(L, t, hf):
                c = 2 * t + hf
                if hf == 0:
                    pe.wait_ge(xb_ready, L * 4 + 2 * t + 2)
                else:
                    pe.wait_ge(st_ready, L * 3 + c)
                rows_ = slice(CHUNK * hf, CHUNK * hf + CHUNK)
                for g in range(2):
                    mm = nc.tensor.matmul(psC[:, g, :], btok[rows_, g, :], xd[rows_, 512 * g:512 * g + 512],
                                          start=True, stop=True)
                mm.then_inc(st_ps, 1)

            def seg_sums(L, t, q):
                if q == 0:
                    pe.wait_ge(off_out, L * 2 + t + 1)
                if q >= 2:
                    pe.wait_ge(dec_mat, L * 8 + 4 * t + q - 1)
                nc.tensor.matmul(psD[:, q % 2, :], ident16,
                                 mask16.rearrange("p (u l) -> p u l", u=1).broadcast_to([P, 4, P]),
                                 start=True, stop=False, skip_group_check=True)
                for hh in range(4):
                    h = 16 * t + 4 * q + hh
                    mm = nc.tensor.matmul(psD[:, q % 2, hh * P:hh * P + P],
                                          small(S_ADT)[:, h:h + 1].broadcast_to([P, P]), tri,
                                          start=False, stop=hh == 3, skip_group_check=True)
                mm.then_inc(seg_ps, 1)

            def diag(L, t, q):
                pe.wait_ge(m_ready, L * 8 + 4 * t + q + 1)
                if t == 0 and q == 0:
                    pe.wait_ge(st_ready, L * 3 + 2)
                if t == 1 and q == 0:
                    wait_uT(L, 4)
                for hh in range(4):
                    h = 4 * q + hh
                    mm = nc.tensor.matmul(psC[:, h // 8, (h % 8) * HD:(h % 8 + 1) * HD], seg[:, q % 2, hh, :],
                                          tm[:, t, h * HD:h * HD + HD], start=True, stop=True)
                mm.then_inc(diag_ps, 1)

            def output_tail(L, c, hi, lo, kt0, outs, under):
                for j in range(4):
                    chunk_ready(L, c + j)
                    mm = k_chunk(L, c + j, 0, hi, lo, kt0 + 2 * j, kt0 + 7, outs)
                mm.then_inc(gemm_t0, 1)
                for j in range(4):
                    k_chunk(L, c + j, 1, hi, lo, kt0 + 2 * j, kt0 + 7, outs, under if j == 2 else None) \
                        .then_inc(w_used, 1)

            pe.wait_ge(ident_in, 16)
            u_transposes(0, 0)
            pe.wait_ge(setup_in, 32)
            nc.tensor.matmul(psD[0:HEADS, 0, 0:REL - 1], table[0:BUCKETS, :],
                             consts[0:BUCKETS, K_ONEHOT:K_ONEHOT + REL - 1], start=True, stop=True).then_inc(bias_ps, 1)
            pe.wait_ge(bias_sb, 1)
            pe.wait_ge(masks_ready, 1)
            with pe.Fori(0, DEPTH) as L:
                ffn(L, 0)
                k_v(L)
                dt_product(L)
                for half in range(2):
                    turned_chunk(L, W_Q, C_Q, half)
                dt_turn(L)
                for half in range(2):
                    turned_chunk(L, W_Q + 1, C_Q + 2, half)
                    attention_step(L, half)
                for k in range(3):
                    for half in range(2):
                        turned_chunk(L, W_XBC + k, C_XBC + 2 * k, half)
                        attention_step(L, 2 + 2 * k + half)
                for half in range(2):
                    for t in range(TT):
                        z_part(L, 0, half, t)
                    attention_step(L, 8 + half)
                    if half == 0:
                        decay_sums(L)
                out2 = {0: gemm[0], 1: gemm[1], "start": (C_OUT_ATT, 0)}

                def out_att(j, t):
                    c = C_OUT_ATT + j
                    if j == 0:
                        pe.wait_ge(win_evac, L * N_WIN + W_Z + t + 1)
                    if t == 0:
                        chunk_ready(L, c)
                    mm = k_chunk(L, c, t, attT_hi, attT_lo, 2 * j, -1, out2)
                    if t == 1:
                        mm.then_inc(w_used, 1)

                def out_ssd(j):
                    c = C_OUT_SSD + j
                    chunk_ready(L, c)
                    return k_chunk(L, c, 0, uT_hi, uT_lo, 2 * j, KT - 1, out2)

                z_part(L, 1, 0, 0)
                ssd_turn(L, 0)
                z_part(L, 1, 0, 1)
                z_part(L, 1, 1, 0)
                ssd_state(L, 0, 0)
                z_part(L, 1, 1, 1)
                ssd_off(L, 0, 1)
                ssd_state(L, 0, 1)
                out_att(0, 0)
                seg_sums(L, 0, 0)
                seg_sums(L, 0, 1)
                out_att(0, 1)
                diag(L, 0, 0)
                seg_sums(L, 0, 2)
                out_att(1, 0)
                diag(L, 0, 1)
                seg_sums(L, 0, 3)
                diag(L, 0, 2)
                out_att(1, 1)
                diag(L, 0, 3)
                out_att(2, 0)
                ssd_turn(L, 1)
                out_att(2, 1)
                out_att(3, 0)
                ssd_off(L, 1, 0)
                ssd_state(L, 1, 0)
                out_att(3, 1)
                ssd_off(L, 1, 1)
                u_transposes(L, 4)
                seg_sums(L, 1, 0)
                seg_sums(L, 1, 1)
                wait_uT(L, 4)
                out_ssd(0)
                diag(L, 1, 0)
                seg_sums(L, 1, 2)
                diag(L, 1, 1)
                seg_sums(L, 1, 3)
                out_ssd(1)
                diag(L, 1, 2)
                diag(L, 1, 3)
                out_ssd(2)
                out_ssd(3).then_inc(gemm_t0, 1)
                u_transposes(L, 5)
                for j in range(4):
                    if j % 2 == 0:
                        wait_uT(L, 5, j // 2)
                    k_chunk(L, C_OUT_SSD + j, 1, uT_hi, uT_lo, 2 * j, KT - 1, out2,
                            (lambda: u_transposes(L, 6)) if j == 2 else None).then_inc(w_used, 1)
                ffn(L, 1)
                chunk_ready(L, C_PLE)
                pe.wait_ge(ple_lo_s, L + 1)
                outp = {0: psC, 1: psD, "start": (C_PLE, 0)}
                k_chunk(L, C_PLE, 1, ple_hi, ple_lo, 0, 1, outp).then_inc(gemm_t0, 1)
                wait_uT(L, 8)
                k_chunk(L, C_PLE, 0, ple_hi, ple_lo, 0, 1, outp).then_inc(w_used, 1)
                outg = {0: gemm[0], 1: gemm[1], "start": (C_GATE, 0)}
                for j in range(4):
                    if j == 1:
                        pe.wait_ge(pw_ready, L * 2 + 1)
                        u_transposes(L, 9)
                    chunk_ready(L, C_GATE + j)
                    mm = k_chunk(L, C_GATE + j, 0, uT_hi, uT_lo, 2 * j, KT - 1, outg)
                mm.then_inc(gemm_t0, 1)
                wait_uT(L, 9)
                for j in range(4):
                    if j == 3:
                        u_transposes(L + 1, 0)
                    k_chunk(L, C_GATE + j, 1, uT_hi, uT_lo, 2 * j, KT - 1, outg).then_inc(w_used, 1)

        @block.scalar
        def _(act):
            def copy(dst, src):
                return nc.scalar.activation(dst, src, ACT.Copy)

            def split(L, c, i=0):
                s = c % RING
                act.wait_ge(stage_full[s], stage_value(L, c, i))
                act.wait_ge(w_used, chunk_value(L, c, i))
                cols = chunk_cols(c)
                copy(w_hi[s][:, cols], stage[s][:, cols]).then_inc(hi_ready, 1)

            def tok0(L, n, i=0):
                act.wait_ge(gemm_t0, L * N_T0 + i + n + 1)

            def tok1(L, c, i=0):
                act.wait_ge(w_used, chunk_value(L, c, i) + RING)

            def square(L, n, src, part=0, to=None):
                if to is None:
                    to = squares[:, n % 6, 512 * part:512 * part + src.shape[1]]
                nc.scalar.activation(to, src, ACT.Square,
                                     accum_out=ss[:, 2 * n + part:2 * n + part + 1]).then_inc(ss_ready, 1)

            def y_square(L, n, t):
                square(L, n, gemm[t][:, 0, :], 0)
                act.wait_ge(y_half, L * N_YH + Y_NTH[n] + 1)
                square(L, n, gemm[t][:, 1, :], 1)

            def u_hi(L, n):
                t = n % 2
                for half in range(2):
                    act.wait_ge(uT_ps, L * N_UT + 2 * n + half + 1)
                    copy(uT_hi[:, 4 * half:4 * half + 4, t * P:t * P + P],
                         turn[t][:, half, :].rearrange("p (k n) -> p k n", n=P)).then_inc(uT_hi_s, 1)

            def x_square(L, n, nx, t):
                act.wait_ge(x_ready, L * N_X + nx + 1)
                square(L, n, x_sb[:, t, :])

            def boundary(L, n0, t0_at, c_next, nx, nu, folded):
                tok0(L, t0_at)
                y_square(L, n0, 0)
                split(L, c_next)
                x_square(L, n0 + 1, nx, 0)
                split(L, c_next + 1)
                u_hi(L, nu)
                split(L, c_next + 2)
                tok1(L, c_next - 1)
                y_square(L, n0 + 2, 1)
                if not folded:
                    x_square(L, n0 + 3, nx + 1, 1)
                    u_hi(L, nu + 1)
                elif nu != 8:
                    u_hi(L, nu + 1)
                    x_square(L, n0 + 3, nx + 1, 1)

            def ffn_gates(L, f, par, g0, i, c):
                for t in range(TT):
                    if t == 0:
                        tok0(L, T0_FFN[f] + g0, i * 2)
                    else:
                        tok1(L, c + 1, i)
                    n = FFN_NORM[f][t]
                    if isinstance(i, int):
                        act.wait_ge(rstd_ready, L * N_NORM + n + 1)
                    nc.scalar.activation(sg[:, par, t, :], gemm[par][:, t, 0:FW], ACT.Silu,
                                         scale=rstd[:, n:n + 1]).then_inc(silu_ready, 1)

            def h_hi(L, f, par, g0, i):
                act.wait_ge(hT_ps, L * N_HT + f * GROUPS + g0 + i * 2 + 1)
                dst = hT_hi_t[:, bass.ds(i * 4 * SEQ + g0 * 2 * SEQ, 2 * SEQ)] if not isinstance(i, int) \
                    else hT_hi_t[:, g0 * 2 * SEQ:(g0 + 1) * 2 * SEQ]
                copy(dst, turn[par][:, 0, :]).then_inc(hT_hi_s, 1)

            def ffn(L, f):
                c0, cd = (C_FFN1, C_FFN2)[f], (C_DOWN1, C_DOWN2)[f]
                split(L, c0 + 3)
                split(L, c0 + 4)
                ffn_gates(L, f, 0, 0, 0, c0)
                with act.Fori(0, (GROUPS - 1) // 2) as i:
                    for par in (1, 0):
                        g0 = 2 - par
                        split(L, c0 + 2 * g0 + 3, i)
                        split(L, c0 + 2 * g0 + 4, i)
                        ffn_gates(L, f, par, g0, i, c0 + 2 * g0)
                        h_hi(L, f, 1 - par, g0 - 1, i)
                split(L, cd + 3)
                h_hi(L, f, 0, GROUPS - 1, 0)
                for j in range(1, GROUPS - 3):
                    split(L, cd + j + 3)

            def attention_step(L, n, c):
                late = n >= N_ITEM
                if 1 <= n <= N_ITEM:
                    act.wait_ge(pT_ps, L * N_ITEM + n)
                    if n >= 3:
                        act.wait_ge(pv_ps, L * N_ITEM + n - 2)
                    copy(pT[:, (n - 1) % 2], psD[:, 0, :]).then_inc(pT_ready, 1)
                if not late:
                    split(L, c)
                if 0 <= n < N_ITEM:
                    b = n % 2
                    sm = att_s[:, 20 * b:20 * b + 20]
                    act.wait_ge(logit_ready, L * N_ITEM + n + 1)
                    for hh in range(4):
                        nc.scalar.activation(lg[:, b, hh, :], lg[:, b, hh, :], ACT.Exp,
                                             bias=sm[:, 4 + hh:5 + hh], accum_out=sm[:, 12 + hh:13 + hh])
                    nc.scalar.activation(sm[:, 8:12], sm[:, 8:12], ACT.Exp).then_inc(exp_ready, 1)
                if 2 <= n <= N_ITEM + 1:
                    m = n - 2
                    t, kv = item(m)
                    act.wait_ge(pv_ps, L * N_ITEM + m + 1)
                    for par in range(2):
                        dst, src = att_views(attT_hi, t, kv, par)
                        last = copy(dst, src)
                    last.then_inc(att_hi_s, 1)
                if late:
                    split(L, c)

            def group_evac(L, k):
                ps = gemm[k % 2]
                if W_Q <= k < W_XBC:
                    last = copy(qT[:, 4 * (k - W_Q):4 * (k - W_Q) + 4, :], ps[:].rearrange("p b (m n) -> p (b m) n", n=SEQ))
                elif k == W_KV:
                    for kv in range(KV):
                        src = ps[HD * (kv % 2):HD * (kv % 2) + HD, 0, SEQ * (kv // 2):SEQ * (kv // 2) + SEQ]
                        for u in range(2):
                            copy(kdup[HD * u:HD * u + HD, kv, :], src)
                    top, low, every = slice(0, CHUNK), slice(CHUNK, P), slice(0, P)
                    for to, w, of, t in ((every, 1, every, 0), (every, 3, every, 1), (low, 0, top, 0),
                                         (top, 2, low, 0), (low, 2, top, 1)):
                        v = ps[of, 1, 256 * t:256 * t + 256].rearrange("p (k u d) -> p k u d", k=KV, u=1)
                        last = copy(vwin[to, w], v.broadcast_to([v.shape[0], KV, 2, HD]))
                elif k >= W_XBC:
                    last = copy(raw[:, 4 * (k - W_XBC):4 * (k - W_XBC) + 4, :],
                                ps[:].rearrange("p b (m n) -> p (b m) n", n=SEQ))
                last.then_inc(win_evac, 1)

            def conv_silu(L, b):
                act.wait_ge(conv_acc, L * 3 + b + 1)
                nc.scalar.activation(raw[:, 4 * b:4 * b + 4, :], conv_sums(b), ACT.Silu).then_inc(conv_ready, 1)

            def z_gate(L, k, t):
                if t == 0:
                    tok0(L, T0_Z + k)
                else:
                    tok1(L, C_Z + 2 * k + 1)
                last = nc.scalar.activation(zs[:, t, 512 * k:512 * k + 512], gemm[(W_Z + k) % 2][:, t, :], ACT.Silu)
                if t == 1:
                    last.then_inc(win_evac, 1)

            def decay_matrices(L, t, q):
                act.wait_ge(seg_ps, L * 8 + 4 * t + q + 1)
                if q >= 2 or t >= 1:
                    act.wait_ge(diag_ps, L * 8 + 4 * t + q - 1)
                for hh in range(4):
                    h = 32 * S_NCS + 16 * t + 4 * q + hh
                    last = nc.scalar.activation(seg[:, q % 2, hh, :], psD[:, q % 2, hh * P:hh * P + P], ACT.Exp,
                                                bias=dts[:, h:h + 1])
                last.then_inc(dec_mat, 1)

            def ssd_square(L, t):
                for half in range(2):
                    w = slice(512 * half, 512 * half + 512)
                    act.wait_ge(yg_ready, L * 4 + 2 * t + half + 1)
                    square(L, 6 + t, xs[:, t, w], half, zs[:, t, w])

            split(0, 0)
            u_hi(0, 0)
            act.wait_ge(bias_ps, 1)
            copy(dts[0:HEADS, 0:REL - 1], psD[0:HEADS, 0, 0:REL - 1]).then_inc(bias_sb, 1)
            split(0, 1)
            with act.Fori(0, DEPTH) as L:
                x_square(L, 0, 0, 0)
                u_hi(L, 1)
                x_square(L, 1, 1, 1)
                split(L, 2)
                ffn(L, 0)
                boundary(L, 2, T0_DOWN[0], C_KV, 2, 2, False)
                act.wait_ge(params_in_s, L * 16 + 16)
                nc.scalar.activation(soft[:], params[:, A_ALOG:A_ALOG + HEADS], ACT.Exp).then_inc(a_ready, 1)
                split(L, C_KV + 3)
                split(L, C_KV + 4)
                tok1(L, C_KV + 1)
                group_evac(L, W_KV)
                tok1(L, C_DT)
                copy(raw[0:HEADS, 0, :], psD[0:HEADS, 0, 0:SEQ]).then_inc(dt_rows, 1)
                split(L, C_DT + 3)
                split(L, C_Q + 3)
                split(L, C_Q + 4)
                tok1(L, C_Q + 1)
                group_evac(L, W_Q)
                act.wait_ge(dt_ps, L + 1)
                copy(small(S_DTR), psC[:, 0, 0:2 * HEADS]).then_inc(dt_ready, 1)
                split(L, C_Q + 5)
                attention_step(L, 0, C_Q + 2 + 4)
                tok1(L, C_Q + 3)
                group_evac(L, W_Q + 1)
                act.wait_ge(dtv_ready, L + 1)
                nc.scalar.activation(small(S_W), small(S_W), ACT.Exp).then_inc(dexp_ready, 1)
                attention_step(L, 1, C_Q + 3 + 4)
                for n in range(2, 8):
                    k = (n - 2) // 2
                    if n % 2:
                        tok1(L, C_XBC + 2 * k + 1)
                        group_evac(L, W_XBC + k)
                    attention_step(L, n, C_XBC + n - 2 + 4)
                    if n == 6:
                        conv_silu(L, 0)
                attention_step(L, 8, C_Z + 4)
                conv_silu(L, 1)
                conv_silu(L, 2)
                act.wait_ge(conv_ready, L * 3 + 3)
                for t in range(TT):
                    z_gate(L, 0, t)
                attention_step(L, 9, C_Z + 5)
                act.wait_ge(cs_ready, L + 1)
                nc.scalar.activation(dts[:, 32 * S_ECS:32 * (S_DEC1 + 1)], dts[:, 32 * S_ECS:32 * (S_DEC1 + 1)],
                                     ACT.Exp).then_inc(dec_ready, 1)
                split(L, C_Z + 6)
                z_gate(L, 1, 0)
                z_gate(L, 1, 1)
                split(L, C_Z + 7)
                decay_matrices(L, 0, 0)
                decay_matrices(L, 0, 1)
                decay_matrices(L, 0, 2)
                split(L, C_OUT_ATT + 4)
                decay_matrices(L, 0, 3)
                split(L, C_OUT_ATT + 5)
                ssd_square(L, 0)
                split(L, C_OUT_ATT + 6)
                u_hi(L, 4)
                decay_matrices(L, 1, 0)
                decay_matrices(L, 1, 1)
                split(L, C_OUT_ATT + 7)
                decay_matrices(L, 1, 2)
                decay_matrices(L, 1, 3)
                ssd_square(L, 1)
                u_hi(L, 5)
                boundary(L, 8, T0_OUT, C_FFN2, 4, 6, True)
                ffn(L, 1)
                act.wait_ge(ple_loaded, L * 16 + 16)
                copy(ple_hi_t[:], ple_raw_t[:]).then_inc(ple_hi_s, 1)
                boundary(L, 12, T0_DOWN[1], C_PLE, 6, 8, True)
                tok0(L, T0_PLE)
                copy(pw[:, 1, :], psD[:].rearrange("p b n -> p (b n)")).then_inc(pw_ready, 1)
                tok1(L, C_PLE)
                copy(pw[:, 0, :], psC[:].rearrange("p b n -> p (b n)")).then_inc(pw_ready, 1)
                split(L, C_PLE + 3)
                u_hi(L, 9)
                x_square(L, 15, 7, 1)
                split(L, C_PLE + 4)
                for t in range(TT):
                    if t == 0:
                        tok0(L, T0_GATE)
                    else:
                        tok1(L, C_GATE + 3)
                    n = (13, 15)[t]
                    act.wait_ge(rstd_ready, L * N_NORM + n + 1)
                    for half in range(2):
                        w = slice(512 * half, 512 * half + 512)
                        nc.scalar.activation(tm[:, t, w], gemm[t][:, half, :], ACT.Sigmoid,
                                             scale=rstd[:, n:n + 1]).then_inc(gate_ready, 1)
                    for half in range(2):
                        w = slice(512 * half, 512 * half + 512)
                        act.wait_ge(gated, L * 4 + 2 * t + half + 1)
                        square(L, 16 + t, pw[:, t, w], half)
                    if t == 0:
                        split(L + 1, 0)
                        split(L + 1, 1)
                        u_hi(L + 1, 0)

        @block.vector
        def _(dve):
            nc.vector.nop().then_inc(lo_ready, RING)

            def split(L, c, i=0):
                s = c % RING
                dve.wait_ge(hi_ready, chunk_value(L, c, i))
                cols = chunk_cols(c)
                nc.vector.tensor_tensor(w_lo[s][:, cols], stage[s][:, cols], w_hi[s][:, cols].bitcast(F32),
                                        ALU.subtract).then_inc(lo_ready, 1)

            def fence():
                dve.drain()

            def wait_rms(L, n):
                dve.wait_ge(rstd_ready, L * N_NORM + n + 1)

            def row_of(L, r):
                if r == 0:
                    return row0
                s = ROW_SLOT[r]
                dve.wait_ge(row_loaded[s], L * (16 * ROW_LOADS[s]) + 16 * ROW_NTH[r])
                return rows[s]

            def update_x(L, n, t):
                wait_rms(L, n)
                nc.vector.scalar_tensor_tensor(x_sb[:, t, :], tm[:, t, :], rstd[:, n:n + 1], x_sb[:, t, :],
                                               ALU.mult, ALU.add).then_inc(x_ready, 1)

            def post(L, n, r, t, step):
                row = row_of(L, r)
                for b in (1, 0):
                    w = slice(512 * b, 512 * b + 512)
                    if b == 0:
                        dve.wait_ge(ss_ready, L * N_SS + SS_DONE[n] - 1)
                    m = nc.vector.scalar_tensor_tensor(tm[:, t, w], gemm[t][:, b, :], step * RMS_D, row[:, w],
                                                       ALU.mult, ALU.mult)
                    if b == 1:
                        m.then_inc(y_half, 1)
                fence()
                update_x(L, n, t)

            def pre(L, n, r, t, src, folded):
                row = row_of(L, r)
                if not folded:
                    nc.vector.scalar_tensor_tensor(tm[:, t, :], src, RMS_D, row[:], ALU.mult, ALU.mult)
                    fence()
                    wait_rms(L, n)
                for half in range(2):
                    w = slice(512 * half, 512 * half + 512)
                    if folded:
                        m = nc.vector.scalar_tensor_tensor(tm[:, t, w], src[:, w], RMS_D, row[:, w], ALU.mult, ALU.mult)
                    else:
                        m = nc.vector.tensor_scalar(tm[:, t, w], tm[:, t, w], rstd[:, n:n + 1], None, ALU.mult)
                    m.then_inc(u_ready, 1)

            def u_lo(L, n):
                t = n % 2
                for half in range(2):
                    dve.wait_ge(uT_hi_s, L * N_UT + 2 * n + half + 1)
                    k = slice(4 * half, 4 * half + 4)
                    nc.vector.tensor_tensor(uT_lo[:, k, t * P:t * P + P],
                                            turn[t][:, half, :].rearrange("p (k n) -> p k n", n=P),
                                            uT_hi[:, k, t * P:t * P + P].bitcast(F32),
                                            ALU.subtract).then_inc(uT_lo_s, 1)

            def boundary(L, n0, t0_at, r_post, r_pre, step, nu, c_next, folded):
                dve.wait_ge(gemm_t0, L * N_T0 + t0_at + 1)
                post(L, n0, r_post, 0, step)
                fence()
                pre(L, n0 + 1, r_pre, 0, x_sb[:, 0, :], folded)
                split(L, c_next)
                split(L, c_next + 1)
                u_lo(L, nu)
                dve.wait_ge(w_used, chunk_value(L, c_next - 1, 0) + RING)
                post(L, n0 + 2, r_post, 1, step)
                fence()
                pre(L, n0 + 3, r_pre, 1, x_sb[:, 1, :], folded)
                if nu != 8:
                    u_lo(L, nu + 1)
                split(L, c_next + 2)

            def products(L, f, par, g0, i):
                for t in range(TT):
                    dve.wait_ge(silu_ready, L * N_H + f * 2 * GROUPS + 2 * g0 + i * 4 + t + 1)
                    n = FFN_NORM[f][t]
                    nc.vector.scalar_tensor_tensor(hs[:, par, t, :], gemm[par][:, t, FW:2 * FW], rstd[:, n:n + 1],
                                                   sg[:, par, t, :], ALU.mult, ALU.mult).then_inc(h_ready, 1)

            def h_lo(L, f, par, g0, i):
                dve.wait_ge(hT_hi_s, L * N_HT + f * GROUPS + g0 + i * 2 + 1)
                at_ = bass.ds(i * 4 * SEQ + g0 * 2 * SEQ, 2 * SEQ) if not isinstance(i, int) \
                    else slice(g0 * 2 * SEQ, (g0 + 1) * 2 * SEQ)
                nc.vector.tensor_tensor(hT_lo_t[:, at_], turn[par][:, 0, :], hT_hi_t[:, at_].bitcast(F32),
                                        ALU.subtract).then_inc(hT_lo_s, 1)

            def ffn(L, f):
                c0, cd = (C_FFN1, C_FFN2)[f], (C_DOWN1, C_DOWN2)[f]
                split(L, c0 + 3)
                split(L, c0 + 4)
                products(L, f, 0, 0, 0)
                with dve.Fori(0, (GROUPS - 1) // 2) as i:
                    for par in (1, 0):
                        g0 = 2 - par
                        split(L, c0 + 2 * g0 + 3, i)
                        split(L, c0 + 2 * g0 + 4, i)
                        products(L, f, par, g0, i)
                        h_lo(L, f, 1 - par, g0 - 1, i)
                split(L, cd + 3)
                h_lo(L, f, 0, GROUPS - 1, 0)
                for j in range(1, GROUPS - 3):
                    split(L, cd + j + 3)

            def attention_step(L, n, c=None):
                if 0 <= n < N_ITEM:
                    t, kv = item(n)
                    b = n % 2
                    sm = att_s[:, 20 * b:20 * b + 20]
                    bs = bias[:, 4 * kv:4 * kv + 4, :].rearrange("p (u k) j -> p u (k j)", u=2)
                    lgu = lg[:, b].rearrange("p (u k) j -> p u (k j)", u=2)
                    sc = psC[:, :, 0:2 * WIN]
                    dve.wait_ge(score_ps, L * N_ITEM + n + 1)
                    if n >= 2:
                        dve.wait_ge(pT_ps, L * N_ITEM + n - 1)
                    if t == 0:
                        nc.vector.memset(lg[0:CHUNK, b, :, 0:CHUNK], MASKED)
                        for u in range(2):
                            nc.vector.scalar_tensor_tensor(
                                lg[0:CHUNK, b, 2 * u:2 * u + 2, CHUNK:],
                                psC[0:CHUNK, u, 0:2 * WIN].rearrange("p (k j) -> p k j", k=2)[:, :, CHUNK:], SCALE,
                                bias[0:CHUNK, 4 * kv + 2 * u:4 * kv + 2 * u + 2, CHUNK:], ALU.mult, ALU.add)
                        nc.vector.scalar_tensor_tensor(lgu[CHUNK:], sc[CHUNK:], SCALE, bs[CHUNK:],
                                                       ALU.mult, ALU.add)
                    else:
                        nc.vector.scalar_tensor_tensor(lgu, sc, SCALE, bs, ALU.mult, ALU.add)
                    fence()
                    sink = params[:, A_SINK + 4 * kv:A_SINK + 4 * kv + 4]
                    nc.vector.tensor_reduce(sm[:, 0:4], lg[:, b], AX, ALU.max)
                    fence()
                    nc.vector.tensor_tensor(sm[:, 0:4], sm[:, 0:4], sink, ALU.max)
                    fence()
                    nc.vector.tensor_scalar(sm[:, 4:8], sm[:, 0:4], -1.0, None, ALU.mult)
                    nc.vector.tensor_tensor(sm[:, 8:12], sink, sm[:, 0:4], ALU.subtract).then_inc(logit_ready, 1)
                if c is not None:
                    split(L, c)
                if 0 <= n < N_ITEM:
                    dve.wait_ge(exp_ready, L * N_ITEM + n + 1)
                    nc.vector.tensor_tensor(sm[:, 12:16], sm[:, 12:16], sm[:, 8:12], ALU.add)
                    fence()
                    nc.vector.reciprocal(sm[:, 16:20], sm[:, 12:16])
                    fence()
                    nc.vector.tensor_tensor(lg[:, b], lg[:, b],
                                            sm[:, 16:20].rearrange("p (h u) -> p h u", u=1)
                                            .broadcast_to([P, 4, WIN]), ALU.mult).then_inc(prob_ready, 1)
                if 2 <= n <= N_ITEM + 1:
                    m = n - 2
                    t, kv = item(m)
                    dve.wait_ge(att_hi_s, L * N_ITEM + m + 1)
                    for par in range(2):
                        dst, src = att_views(attT_lo, t, kv, par)
                        hi, _ = att_views(attT_hi, t, kv, par)
                        last = nc.vector.tensor_tensor(dst, src, hi.bitcast(F32), ALU.subtract)
                    last.then_inc(att_lo_s, 1)

            def conv(L, b, part):
                if part == 0:
                    dve.wait_ge(win_evac, L * N_WIN + W_XBC + b + 1)
                    dve.wait_ge(conv_ready, L * 3 + 1)
                a = conv_sums(b)
                two = (2 * part, 2 * part + 1)
                for k in two:
                    ct = 4 * b + k
                    nc.vector.tensor_scalar(a[:, k, :], raw[:, ct, :],
                                            params[:, A_CW + 4 * ct + 3:A_CW + 4 * ct + 4],
                                            params[:, A_CB + ct:A_CB + ct + 1], ALU.mult, ALU.add)
                for tap in (2, 1, 0):
                    fence()
                    d = CONVW - 1 - tap
                    if part and tap == 0:
                        dve.wait_ge(conv_acc, L * 3 + b)
                    for k in two:
                        ct = 4 * b + k
                        w = params[:, A_CW + 4 * ct + tap:A_CW + 4 * ct + tap + 1]
                        last = nc.vector.scalar_tensor_tensor(a[:, k, d:], raw[:, ct, :SEQ - d], w, a[:, k, d:],
                                                              ALU.mult, ALU.add)
                if part:
                    last.then_inc(conv_acc, 1)

            def over_heads(ap16, n=HD):
                return ap16.rearrange("p (h u) -> p h u", u=1).broadcast_to([P, ap16.shape[1], n])

            def dt_front(L):
                dve.wait_ge(dt_ready, L + 1)
                r2 = small(S_DTR).rearrange("p (t h) -> p t h", t=TT)
                v2 = small(S_V).rearrange("p (t h) -> p t h", t=TT)
                for t in range(TT):
                    nc.vector.tensor_tensor(v2[:, t, :], r2[:, t, :], params[:, A_DTB:A_DTB + HEADS], ALU.add)
                fence()
                nc.vector.tensor_scalar(small(S_DT), small(S_V), 0.0, None, ALU.max)
                nc.vector.tensor_scalar(small(S_W), small(S_V), -1.0, None, ALU.mult)
                fence()
                nc.vector.tensor_tensor(small(S_W), small(S_W), small(S_V), ALU.min).then_inc(dtv_ready, 1)

            def dt_ratio(L):
                dve.wait_ge(dexp_ready, L + 1)
                nc.vector.tensor_scalar(small(S_NCS), small(S_W), 2.0, None, ALU.add)
                fence()
                nc.vector.reciprocal(small(S_DTR), small(S_NCS))
                fence()
                nc.vector.tensor_tensor(small(S_DTR), small(S_DTR), small(S_W), ALU.mult).then_inc(ratio_ready, 1)

            def decays(L):
                dve.wait_ge(cs_ps, L + 1)
                nc.vector.tensor_scalar(small(S_NCS), psC[:, 0, 0:32], -1.0, None, ALU.mult)
                nc.vector.tensor_copy(small(S_ECS), psC[:, 0, 0:32])
                nc.vector.tensor_copy(dts[:, 32 * S_DEC0:32 * S_DEC0 + 64], psC[:, 0, 64:128])
                fence()
                nc.vector.tensor_tensor(small(S_EDEC), psC[:, 0, 32:64], small(S_NCS), ALU.add) \
                    .then_inc(cs_ready, 1)

            def heads(ap):
                return ap.rearrange("p (h d) -> p h d", d=HD)

            def half_of(i, t):
                return dts[:, 32 * i + 16 * t:32 * i + 16 * t + 16]

            def ssd_inputs(L, t):
                dve.wait_ge(xT_ps, L * 2 + t + 1)
                if t == 0:
                    dve.wait_ge(dec_ready, L + 1)
                xps = psC[:].rearrange("p b n -> p (b n)")
                nc.vector.tensor_tensor(heads(tm[:, t, :]), heads(xps), over_heads(half_of(S_DT, t)), ALU.mult)
                nc.vector.tensor_tensor(heads(xs[:, t, :]), heads(xps),
                                        over_heads(params[:, A_DSKIP:A_DSKIP + HEADS]), ALU.mult)
                nc.vector.tensor_copy(btok, psD[:, 0, 0:256].rearrange("p (g n) -> p g n", g=2))
                fence()
                nc.vector.tensor_tensor(heads(xd), heads(tm[:, t, :]), over_heads(half_of(S_EDEC, t)), ALU.mult) \
                    .then_inc(xb_ready, 1)
                dve.wait_ge(cb_ps, L * 2 + t + 1)
                nc.vector.tensor_tensor(cbm, psD[:, 1, 0:256].rearrange("p (g n) -> p g n", g=2),
                                        tri.rearrange("p (u n) -> p u n", u=1).broadcast_to([P, 2, P]),
                                        ALU.mult).then_inc(xb_ready, 1)

            def ssd_states(L, t, halves=(0, 1)):
                for hf in halves:
                    c = 2 * t + hf
                    if c >= 1:
                        r = slice(CHUNK * hf, CHUNK * hf + CHUNK)
                        dve.wait_ge(off_ps, L * 3 + c)
                        last = nc.vector.tensor_tensor(
                            heads(acc)[r], heads(psD[:].rearrange("p b n -> p (b n)"))[r],
                            over_heads(half_of(S_ECS, t))[r], ALU.mult)
                        if hf:
                            last.then_inc(off_out, 1)
                    if c < 3:
                        dve.wait_ge(st_ps, L * 3 + c + 1)
                        sps = psC[:].rearrange("p b n -> p (b n)")
                        if c == 0:
                            nc.vector.tensor_copy(hst, sps).then_inc(st_ready, 1)
                        else:
                            nc.vector.tensor_tensor(heads(hst), heads(hst),
                                                    over_heads(half_of(S_DEC0 + hf, t)), ALU.mult)
                            fence()
                            nc.vector.tensor_tensor(hst, hst, sps, ALU.add).then_inc(st_ready, 1)
                if 1 not in halves:
                    return
                fence()
                r = slice(CHUNK if t == 0 else 0, P)
                nc.vector.tensor_tensor(xs[r, t, :], xs[r, t, :], acc[r, :], ALU.add)

            def mixed(L, t, q):
                b = q % 2
                dve.wait_ge(dec_mat, L * 8 + 4 * t + q + 1)
                nc.vector.tensor_tensor(seg[:, b], seg[:, b],
                                        cbm[:, q // 2, :].rearrange("p (u l) -> p u l", u=1)
                                        .broadcast_to([P, 4, P]), ALU.mult).then_inc(m_ready, 1)

            def ssd_output(L, t, half):
                w = slice(512 * half, 512 * half + 512)
                dve.wait_ge(diag_ps, L * 8 + 4 * t + 2 * half + 2)
                nc.vector.tensor_tensor(xs[:, t, w], psC[:, half, :], xs[:, t, w], ALU.add)
                fence()
                nc.vector.tensor_tensor(xs[:, t, w], xs[:, t, w], zs[:, t, w], ALU.mult).then_inc(yg_ready, 1)

            def ssd_norm(L, t):
                fence()
                pre(L, 6 + t, ROW_SSM, t, xs[:, t, :], False)

            dve.wait_ge(x_in_s[0], 16)
            nc.vector.nop().then_inc(x_ready, 1)
            dve.wait_ge(row0_first, 16)
            pre(0, 0, 0, 0, x_sb[:, 0, :], True)
            split(0, 0)
            u_lo(0, 0)
            dve.wait_ge(ident_in, 16)
            dve.wait_ge(setup_in, 32)
            nc.vector.tensor_copy(ident16, ident)
            nc.vector.tensor_scalar(mask16, tri, 1.0, -MASKED, ALU.subtract, ALU.mult).then_inc(masks_ready, 1)
            split(0, 1)
            dve.wait_ge(x_in_s[1], 16)
            nc.vector.nop().then_inc(x_ready, 1)
            with dve.Fori(0, DEPTH) as L:
                fence()
                pre(L, 1, 0, 1, x_sb[:, 1, :], True)
                u_lo(L, 1)
                split(L, 2)
                ffn(L, 0)
                boundary(L, 2, T0_DOWN[0], 1, 2, 0.5, 2, C_KV, False)
                dve.wait_ge(params_in_s, L * 16 + 16)
                nc.vector.memset(vwin[0:CHUNK, 0], 0.0)
                dve.wait_ge(bias_loaded, 32)
                for c in range(C_KV, C_Q + 2):
                    split(L, c + 3)
                dt_front(L)
                split(L, C_Q + 5)
                attention_step(L, 0, C_Q + 2 + 4)
                dt_ratio(L)
                attention_step(L, 1, C_Q + 3 + 4)
                for n in range(2, 8):
                    attention_step(L, n, C_XBC + n - 2 + 4)
                conv(L, 2, 0)
                attention_step(L, 8)
                conv(L, 2, 1)
                decays(L)
                split(L, C_Z + 4)
                attention_step(L, 9)
                ssd_inputs(L, 0)
                split(L, C_Z + 5)
                ssd_states(L, 0, (0,))
                split(L, C_Z + 6)
                ssd_states(L, 0, (1,))
                split(L, C_Z + 7)
                mixed(L, 0, 0)
                mixed(L, 0, 1)
                mixed(L, 0, 2)
                ssd_output(L, 0, 0)
                split(L, C_OUT_ATT + 4)
                mixed(L, 0, 3)
                ssd_output(L, 0, 1)
                split(L, C_OUT_ATT + 5)
                ssd_inputs(L, 1)
                ssd_norm(L, 0)
                ssd_states(L, 1)
                u_lo(L, 4)
                mixed(L, 1, 0)
                mixed(L, 1, 1)
                split(L, C_OUT_ATT + 6)
                split(L, C_OUT_ATT + 7)
                mixed(L, 1, 2)
                ssd_output(L, 1, 0)
                mixed(L, 1, 3)
                ssd_output(L, 1, 1)
                ssd_norm(L, 1)
                u_lo(L, 5)
                boundary(L, 8, T0_OUT, 3, 4, 1.0, 6, C_FFN2, True)
                ffn(L, 1)
                dve.wait_ge(ple_hi_s, L + 1)
                nc.vector.tensor_tensor(ple_lo_t[:], ple_raw_t[:], ple_hi_t[:].bitcast(F32), ALU.subtract) \
                    .then_inc(ple_lo_s, 1)
                boundary(L, 12, T0_DOWN[1], 5, 6, 0.5, 8, C_PLE, True)
                split(L, C_PLE + 3)
                u_lo(L, 9)
                split(L, C_PLE + 4)
                for t in range(TT):
                    for half in range(2):
                        w = slice(512 * half, 512 * half + 512)
                        dve.wait_ge(gate_ready, L * 4 + 2 * t + half + 1)
                        nc.vector.tensor_tensor(pw[:, t, w], pw[:, t, w], tm[:, t, w], ALU.mult).then_inc(gated, 1)
                    fence()
                    nc.vector.scalar_tensor_tensor(tm[:, t, :], pw[:, t, :], RMS_D, row_of(L, 7)[:],
                                                   ALU.mult, ALU.mult)
                    fence()
                    if t == 0:
                        update_x(L, 16 + t, t)
                    else:
                        wait_rms(L, 17)
                        for half in range(2):
                            w = slice(512 * half, 512 * half + 512)
                            nc.vector.scalar_tensor_tensor(x_sb[:, 1, w], tm[:, 1, w], rstd[:, 17:18], x_sb[:, 1, w],
                                                           ALU.mult, ALU.add).then_inc(x_ready if half else x_half, 1)
                    if t == 0:
                        fence()
                        dve.wait_ge(row0_loaded, L * 16 + 16)
                        pre(L + 1, 0, 0, 0, x_sb[:, 0, :], True)
                        split(L + 1, 0)
                        u_lo(L + 1, 0)
                        split(L + 1, 1)


def buckets():
    rel = np.arange(WIN + CHUNK - 1) - WIN + 1
    nb = BUCKETS // 2
    ret = (rel > 0).astype(np.int32) * nb
    n = np.abs(rel)
    exact = nb // 2
    large = exact + (np.log(np.maximum(n, 1) / exact) / np.log(WIN / exact) * (nb - exact)).astype(np.int32)
    return ret + np.where(n < exact, n, np.minimum(large, nb - 1))


def constants():
    k = np.arange(P)
    same = (k[:, None] // CHUNK) == (k[None, :] // CHUNK)
    c = np.zeros((P, K_ALL), np.float32)
    c[:, K_ID:K_ID + P] = np.eye(P)
    c[:, K_TRI:K_TRI + P] = same & (k[:, None] <= k[None, :])
    c[:, K_BLK:K_BLK + P] = same
    c[:, K_HALF] = k < CHUNK
    c[:, K_HALF + 1] = k >= CHUNK
    c[buckets(), K_ONEHOT + np.arange(WIN + CHUNK - 1)] = 1.0
    return c


def lay_out(ffn1_w13, ffn1_w2, ffn2_w13, ffn2_w2, w_in, w_out, ple_w_gate, ple_w_proj):
    out = np.zeros((DEPTH, CHUNKS, P, CW), np.float32)

    def wide(dst, w, cols):
        m = w[:, :, cols].reshape(DEPTH, 2, 4, P, 512).transpose(0, 1, 3, 2, 4)
        out[:, dst:dst + 2] = m.reshape(DEPTH, 2, P, CW)

    def tall(dst, w):
        n = w.shape[1] // (2 * P)
        m = w.reshape(DEPTH, n, 2, P, D).transpose(0, 1, 3, 2, 4)
        out[:, dst:dst + n] = m.reshape(DEPTH, n, P, CW)

    for c0, w in ((C_FFN1, ffn1_w13), (C_FFN2, ffn2_w13)):
        for g in range(GROUPS):
            a = np.arange(g * FW, (g + 1) * FW)
            wide(c0 + 2 * g, w, np.concatenate([a, a + D_FF]))
    tall(C_DOWN1, ffn1_w2)
    tall(C_DOWN2, ffn2_w2)
    z0, xbc0, dt0, q0, k0 = 0, D, D + 1536, D + 1536 + HEADS, 2 * D + 1536 + HEADS
    for k in range(2):
        wide(C_Q + 2 * k, w_in, np.arange(q0 + 512 * k, q0 + 512 * (k + 1)))
        wide(C_Z + 2 * k, w_in, np.arange(z0 + 512 * k, z0 + 512 * (k + 1)))
    wide(C_KV, w_in, np.arange(k0, k0 + 512))
    for k in range(3):
        wide(C_XBC + 2 * k, w_in, np.arange(xbc0 + 512 * k, xbc0 + 512 * (k + 1)))
    dt = w_in[:, :, dt0:dt0 + HEADS].reshape(DEPTH, KT, P, HEADS).transpose(0, 2, 1, 3)
    out[:, C_DT, :, :KT * HEADS] = dt.reshape(DEPTH, P, KT * HEADS)
    tall(C_OUT_ATT, w_out[:, D:])
    tall(C_OUT_SSD, w_out[:, :D])
    tall(C_PLE, ple_w_proj)
    tall(C_GATE, ple_w_gate)
    return out.reshape(DEPTH * CHUNKS * P, CW)


def kernel(x, p, norm_w, ffn1_w13, ffn1_w2, ffn2_w13, ffn2_w2, w_in, conv_w, conv_b, dt_bias, a_log, d_skip,
           ssm_norm_w, attn_sinks, rel_bias_table, w_out, ple_w_gate, ple_w_proj):
    import concourse.bacc as bacc
    from concourse.bass_utils import run_bass_kernel_spmd

    f = lambda a: np.asarray(a)
    rows = np.concatenate([f(norm_w), f(ssm_norm_w)[:, None]], axis=1).reshape(DEPTH * (NORMS + 1), D)
    rows = np.concatenate([rows, np.zeros((1, D), np.float32)])
    params = np.zeros((DEPTH, P, A_ALL), np.float32)
    params[:, :, A_CW:A_CW + 48] = f(conv_w).reshape(DEPTH, CONVW, CT, P).transpose(0, 3, 2, 1).reshape(DEPTH, P, 48)
    params[:, :, A_CB:A_CB + CT] = f(conv_b).reshape(DEPTH, CT, P).transpose(0, 2, 1)
    sinks = f(attn_sinks).reshape(DEPTH, KV, 2, 2).transpose(0, 1, 3, 2).reshape(DEPTH, HEADS)
    for at, a in ((A_DTB, dt_bias), (A_ALOG, a_log), (A_DSKIP, d_skip), (A_SINK, sinks)):
        params[:, :, at:at + HEADS] = f(a)[:, None, :]
    arrays = {
        "x": f(x).reshape(SEQ, D),
        "chunks": lay_out(*(f(a) for a in (ffn1_w13, ffn1_w2, ffn2_w13, ffn2_w2, w_in, w_out,
                                           ple_w_gate, ple_w_proj))),
        "ple": np.ascontiguousarray(f(p).reshape(DEPTH, SEQ, PLE).transpose(0, 2, 1)).reshape(DEPTH * PLE, SEQ),
        "rows": np.ascontiguousarray(rows),
        "params": params.reshape(DEPTH * P, A_ALL),
        "table": np.ascontiguousarray(
            f(rel_bias_table).reshape(BUCKETS, KV, 2, 2).transpose(0, 1, 3, 2)).reshape(BUCKETS, HEADS),
        "consts": constants(),
    }
    nc = bacc.Bacc("TRN2", target_bir_lowering=False, num_devices=1, dynamic_dma_scratch_size=4096)
    args = [nc.dram_tensor(f"in_{n}", a.shape, mybir.dt.from_np(a.dtype), kind="ExternalInput").ap()
            for n, a in arrays.items()]
    args.append(nc.dram_tensor("rel_bias", (CHUNK * (HEADS * REL + 1),), F32, kind="Internal").ap())
    args.append(nc.dram_tensor("out_x", (SEQ, D), F32, kind="ExternalOutput").ap())
    trunk(nc, *args)
    r = run_bass_kernel_spmd(nc, [{f"in_{n}": a for n, a in arrays.items()}], core_ids=[0])
    return r.results[0]["out_x"].reshape(1, SEQ, D)
```
